# Optimizing a Trainium2 kernel written in Bass

```python
import jax, jax.numpy as jnp
from jax import lax
import numpy as np

D_MODEL = 2048
BATCH = 1
SEQ = 256
DEPTH = 1

CHUNK = 64
EPS = 1e-6
N_MOD = 6
LRU_WIDTH = 1024
LRU_HEADS = 16
LRU_HEAD_DIM = LRU_WIDTH // LRU_HEADS
LRU_CONV = 4
LRU_C = 8.0
SC_WIDTH = 1024
SC_K = 3
POOL_WIDTH = 1024
POOL_WINDOWS = (2, 4, 8, 16)
POOL_GROUPS = 4
POOL_GROUP_DIM = POOL_WIDTH // POOL_GROUPS
POOL_OUT_DIM = D_MODEL // POOL_GROUPS
N_BRANCH = 3
IN_WIDTHS = (LRU_WIDTH, LRU_WIDTH, SC_WIDTH, SC_WIDTH, SC_WIDTH, POOL_WIDTH, N_BRANCH * D_MODEL)
IN_WIDTH = 2 * LRU_WIDTH + 3 * SC_WIDTH + POOL_WIDTH + N_BRANCH * D_MODEL
D_FF = -(-8 * D_MODEL // (3 * 256)) * 256

kernel_name = "hybrid_rglru_shortconv_pool_adaln_block"

def rms_norm(x, gain):
    x32 = x.astype(jnp.float32)
    y = x32 * lax.rsqrt(jnp.mean(x32 * x32, axis=-1, keepdims=True) + EPS)
    return (y * gain.astype(jnp.float32)).astype(x.dtype)

def causal_depthwise_conv(u, w):
    k, ch = w.shape
    return lax.conv_general_dilated(
        u, w[:, None, :].astype(u.dtype), window_strides=(1,), padding=((k - 1, 0),),
        dimension_numbers=("NWC", "WIO", "NWC"), feature_group_count=ch)

def _linear_recurrence_combine(left, right):
    a1, b1 = left
    a2, b2 = right
    return a1 * a2, a2 * b1 + b2

def rglru_branch(u_x, u_gate, conv_w, conv_b, w_a, b_a, w_x, b_x, lam, w_out):
    bsz, s, _ = u_x.shape
    xc = (causal_depthwise_conv(u_x, conv_w) + conv_b).astype(jnp.float32)
    xh = xc.reshape(bsz, s, LRU_HEADS, LRU_HEAD_DIM)
    r = jax.nn.sigmoid(jnp.einsum("bshi,hij->bshj", xh, w_a.astype(jnp.float32)).reshape(bsz, s, LRU_WIDTH) + b_a)
    i = jax.nn.sigmoid(jnp.einsum("bshi,hij->bshj", xh, w_x.astype(jnp.float32)).reshape(bsz, s, LRU_WIDTH) + b_x)
    log_a = -LRU_C * r * jax.nn.softplus(-lam.astype(jnp.float32))
    a = jnp.exp(log_a)
    mult = jnp.sqrt(-jnp.expm1(2.0 * log_a))
    mult = jnp.where((jnp.arange(s) == 0)[None, :, None], 1.0, mult)
    b = mult * (i * xc)
    _, h = lax.associative_scan(_linear_recurrence_combine, (a, b), axis=1)
    y = h * jax.nn.gelu(u_gate.astype(jnp.float32))
    return y.astype(u_x.dtype) @ w_out

def shortconv_branch(u_b, u_c, u_x, conv_w, w_out):
    v = causal_depthwise_conv(u_c * u_x, conv_w)
    return (u_b * v) @ w_out

def pool_branch(u, w_group, scale):
    bsz, s, _ = u.shape
    u32 = u.astype(jnp.float32)
    cs = jnp.pad(jnp.cumsum(u32, axis=1), ((0, 0), (1, 0), (0, 0)))
    t = jnp.arange(s)
    outs = []
    for g, w in enumerate(POOL_WINDOWS):
        sl = slice(g * POOL_GROUP_DIM, (g + 1) * POOL_GROUP_DIM)
        hi = cs[:, 1:, sl]
        lo = jnp.pad(cs[:, : s + 1 - w, sl], ((0, 0), (w - 1, 0), (0, 0)))
        cnt = jnp.minimum(t + 1, w).astype(jnp.float32)[None, :, None]
        outs.append((hi - lo) / cnt - u32[:, :, sl])
    pooled = jnp.stack(outs, axis=2).astype(u.dtype)
    y = jnp.einsum("bsgi,gio->bsgo", pooled, w_group).reshape(bsz, s, D_MODEL)
    return y * scale

def setup_inputs(seed: int = 0) -> dict:
    key = jax.random.key(seed)
    ks = jax.random.split(key, 32)

    def nrm(k, shape, scale):
        return jax.random.normal(k, shape, jnp.float32) * scale

    u = jax.random.uniform(ks[13], (DEPTH, LRU_WIDTH), jnp.float32, 0.9, 0.999)
    sig = u ** (1.0 / LRU_C)
    lru_lambda = jnp.log(sig) - jnp.log1p(-sig)
    return {
        "x": nrm(ks[0], (BATCH, SEQ, D_MODEL), 1.0),
        "c": nrm(ks[1], (BATCH, D_MODEL), 1.0),
        "w_mod": nrm(ks[2], (DEPTH, D_MODEL, N_MOD * D_MODEL), 0.5 * D_MODEL ** -0.5),
        "b_mod": nrm(ks[3], (DEPTH, N_MOD * D_MODEL), 0.02),
        "norm_mix": 1.0 + nrm(ks[4], (DEPTH, D_MODEL), 0.05),
        "w_in": nrm(ks[5], (DEPTH, D_MODEL, IN_WIDTH), D_MODEL ** -0.5),
        "lru_conv_w": nrm(ks[6], (DEPTH, LRU_CONV, LRU_WIDTH), LRU_CONV ** -0.5),
        "lru_conv_b": nrm(ks[7], (DEPTH, LRU_WIDTH), 0.01),
        "lru_w_a": nrm(ks[8], (DEPTH, LRU_HEADS, LRU_HEAD_DIM, LRU_HEAD_DIM), LRU_HEAD_DIM ** -0.5),
        "lru_b_a": nrm(ks[9], (DEPTH, LRU_WIDTH), 0.01),
        "lru_w_x": nrm(ks[10], (DEPTH, LRU_HEADS, LRU_HEAD_DIM, LRU_HEAD_DIM), LRU_HEAD_DIM ** -0.5),
        "lru_b_x": nrm(ks[11], (DEPTH, LRU_WIDTH), 0.01),
        "lru_lambda": lru_lambda,
        "lru_w_out": nrm(ks[12], (DEPTH, LRU_WIDTH, D_MODEL), LRU_WIDTH ** -0.5),
        "sc_conv_w": nrm(ks[14], (DEPTH, SC_K, SC_WIDTH), SC_K ** -0.5),
        "sc_w_out": nrm(ks[15], (DEPTH, SC_WIDTH, D_MODEL), SC_WIDTH ** -0.5),
        "pool_w": nrm(ks[16], (DEPTH, POOL_GROUPS, POOL_GROUP_DIM, POOL_OUT_DIM), POOL_GROUP_DIM ** -0.5),
        "pool_scale": 1.0 + nrm(ks[17], (DEPTH, D_MODEL), 0.1),
        "w_o": nrm(ks[18], (DEPTH, D_MODEL, D_MODEL), D_MODEL ** -0.5),
        "norm_ffn": 1.0 + nrm(ks[19], (DEPTH, D_MODEL), 0.05),
        "ffn_w1": nrm(ks[20], (DEPTH, D_MODEL, D_FF), D_MODEL ** -0.5),
        "ffn_w3": nrm(ks[21], (DEPTH, D_MODEL, D_FF), D_MODEL ** -0.5),
        "ffn_w2": nrm(ks[22], (DEPTH, D_FF, D_MODEL), D_FF ** -0.5),
        "norm_final": 1.0 + nrm(ks[23], (D_MODEL,), 0.05),
    }

def reference(x, c, w_mod, b_mod, norm_mix, w_in, lru_conv_w, lru_conv_b, lru_w_a, lru_b_a, lru_w_x, lru_b_x,
              lru_lambda, lru_w_out, sc_conv_w, sc_w_out, pool_w, pool_scale, w_o, norm_ffn, ffn_w1, ffn_w3,
              ffn_w2, norm_final):
    bsz, s, _ = x.shape
    split_at = np.cumsum(IN_WIDTHS)[:-1].tolist()
    cond = jax.nn.silu(c)
    for l in range(DEPTH):
        mod = (cond @ w_mod[l] + b_mod[l])[:, None, :]
        sh1, sc1, g1, sh2, sc2, g2 = jnp.split(mod, N_MOD, axis=-1)

        h = rms_norm(x, norm_mix[l]) * (1.0 + sc1) + sh1
        p = h @ w_in[l]
        lru_x, lru_g, sc_b, sc_c, sc_x, pool_u, gate_logits = jnp.split(p, split_at, axis=-1)
        y_lru = rglru_branch(lru_x, lru_g, lru_conv_w[l], lru_conv_b[l], lru_w_a[l], lru_b_a[l],
                             lru_w_x[l], lru_b_x[l], lru_lambda[l], lru_w_out[l])
        y_sc = shortconv_branch(sc_b, sc_c, sc_x, sc_conv_w[l], sc_w_out[l])
        y_pool = pool_branch(pool_u, pool_w[l], pool_scale[l])
        gates = jax.nn.sigmoid(gate_logits).reshape(bsz, s, N_BRANCH, D_MODEL)
        merged = gates[:, :, 0] * y_lru + gates[:, :, 1] * y_sc + gates[:, :, 2] * y_pool
        x = x + g1 * (merged @ w_o[l])

        h2 = rms_norm(x, norm_ffn[l]) * (1.0 + sc2) + sh2
        ff = (jax.nn.silu(h2 @ ffn_w1[l]) * (h2 @ ffn_w3[l])) @ ffn_w2[l]
        x = x + g2 * ff
    return rms_norm(x, norm_final)


_drawn_inputs = setup_inputs


def setup_inputs(seed=0):
    import zlib

    import numpy as np

    out = dict(_drawn_inputs(seed))
    spreads = {}
    factors = {'norm_mix': 2.722,
     'lru_conv_b': 8.0,
     'lru_b_a': 64.0,
     'lru_b_x': 64.0,
     'pool_scale': 3.773,
     'norm_ffn': 3.96}
    for name, (base, spread) in spreads.items():
        noise = np.random.default_rng([zlib.crc32(name.encode()), seed]).standard_normal(out[name].shape)
        drawn = base * np.exp(spread * noise) if base else spread * noise
        out[name] = __import__('jax').numpy.asarray(drawn.astype(out[name].dtype))
    for name, factor in factors.items():
        out[name] = (out[name] * factor).astype(out[name].dtype)
    return out
```

```python
from contextlib import ExitStack

import concourse.bass as bass
from concourse import mybir

F32 = mybir.dt.float32
F32R = mybir.dt.float32r
ALU = mybir.AluOpType
ACT = mybir.ActivationFunctionType
AX = mybir.AxisListType

P = 128
D = 2048
S = 256
FF = 5632
EPS = 1e-6
KT = D // P
TOK = S // P
W_LRU = 1024
BT = W_LRU // P
CHUNK = 1024
GROUP = 4
RING = 4
MOD_RING = 4
POOL_WINDOWS = (2, 4, 8, 16)

G_CHUNKS = KT // 2
OUT_CHUNKS = BT // 2
A_GROUPS = 10
PROJ = 0
LRU_OUT = PROJ + A_GROUPS * G_CHUNKS
PAIR = G_CHUNKS + OUT_CHUNKS
POOL_IN = LRU_OUT + 4 * PAIR
SC_OUT = POOL_IN + 2 * G_CHUNKS
POOL_OUT = SC_OUT + 4 * PAIR
POOL_PAIR = G_CHUNKS + 1
W_O = POOL_OUT + 4 * POOL_PAIR
HALF_O = KT
PASSES = (6, 5)
FFN = []
_n = W_O + 2 * HALF_O
for _g in PASSES:
    FFN.append((_n, _n + _g * 2 * G_CHUNKS))
    _n = FFN[-1][1] + 2 * GROUP * _g
N_CHUNKS = _n
MOD_HALF = KT
MOD_ORDER = (1, 0, 2, 3, 4, 5)
N_MOD = 2 * MOD_HALF * len(MOD_ORDER)

P_BMOD = 0
P_NMIX = 96
P_NFFN = 112
P_PSCALE = 128
P_CONVW = 144
P_CONVB = 176
P_BA = 184
P_BX = 192
P_LAM = 200
P_SCW = 208
P_C = 232
N_PARAM = 248

SIDE = ["x0", "x1", "x2", "x3", "m0", "m1", "m2", "m3", "r0", "r1", "i0", "i1", "m4", "m5", "m6", "m7",
        "m8", "m9", "wide_o", "m10", "m11", "wide_f0", "wide_f1"]


def side_use(task):
    uses, done, turn = [0, 0], [0, 0], 0
    for t in SIDE:
        if t.startswith("wide"):
            if t == task:
                return uses[0]
            uses = [uses[0] + 1, uses[1] + 1]
            continue
        if t == task:
            return 2 + turn, uses[turn], done[turn] + 1
        uses[turn] += 1
        done[turn] += 1
        turn = 1 - turn
    raise KeyError(task)


def trunk_kernel(nc, x, params, gate_w, rows, pool_cnt, w_stream, m_stream, ident_in, out):
    with ExitStack() as ctx:

        def sb(name, cols, dt=F32, at=None):
            return ctx.enter_context(nc.sbuf_tensor(name, [P, cols], dt)) if at is None else \
                nc.alloc_sbuf_tensor_at(name, [P, cols], dt, offset=at)

        def sem(name):
            return ctx.enter_context(nc.semaphore(name))

        raw = [sb(f"raw{i}", CHUNK) for i in range(RING)]
        w_hi = [sb(f"w_hi{i}", CHUNK, F32R) for i in range(RING)]
        w_lo = [sb(f"w_lo{i}", CHUNK, F32R) for i in range(RING)]
        mod_raw = [sb(f"mod_raw{i}", CHUNK) for i in range(MOD_RING)]
        h_hi = sb("h_hi", KT * S, F32R)
        h_lo = sb("h_lo", KT * S, F32R)
        mod_acc = [sb(f"mod_acc{i}", CHUNK) for i in range(2)]
        g1_row = sb("g1_row", D)
        g2_row = sb("g2_row", D)
        par = sb("par", N_PARAM)
        modc = sb("modc", 4 * KT)
        aff = sb("aff", 4 * KT)
        silu_c = sb("silu_c", KT)
        sp = sb("sp", 8 * BT)
        stat = sb("stat", 16)
        ident = sb("ident", P)
        ones = sb("ones", P)
        cnt = sb("cnt", sum(POOL_WINDOWS))

        SLOT = D * 4
        r0 = -(-nc.sbuf_base // 64) * 64
        assert r0 + 10 * SLOT <= nc.sbuf_usable_end

        def place(name, slot, cols, dt=F32):
            return nc.alloc_sbuf_tensor_at(name, [P, cols], dt, offset=r0 + int(slot * SLOT))

        x_tok = place("x_tok", 0, TOK * D)
        xn = place("xn", 2, KT * S)
        sq_junk = place("sq_junk", 4, D)
        lx = place("lx", 0, BT * S)
        xc = place("xc", 1, BT * S)
        lr = place("lr", 2, BT * S)
        li = place("li", 3, BT * S)
        lg = place("lg", 4, BT * S)
        w_ga = place("w_ga", 9, BT * P)
        w_gx = place("w_gx", 9.5, BT * P)
        lru_hi = place("lru_hi", 1, BT * S, F32R)
        lru_lo = place("lru_lo", 2, BT * S, F32R)
        sb_ = place("sb_", 6, BT * S)
        sc_ = place("sc_", 5, BT * S)
        sv = place("sv", 0, BT * S)
        sc_hi = place("sc_hi", 3, BT * S, F32R)
        sc_lo = place("sc_lo", 4, BT * S, F32R)
        merged = place("merged", 7, KT * S)
        gate = place("gate", 9, GROUP * S)
        term = place("term", 9.5, GROUP * S)
        pu = place("pu", 5, BT * S)
        pa = place("pa", 6, BT * S)
        pb = place("pb", 0, BT * S)
        pool_hi = place("pool_hi", 1, BT * S, F32R)
        pool_lo = place("pool_lo", 2, BT * S, F32R)
        mg_hi = place("mg_hi", 3, KT * S, F32R)
        mg_lo = place("mg_lo", 5, KT * S, F32R)
        res = place("res", 1, TOK * D)
        nf_row = place("nf_row", 0, D)
        xn2 = place("xn2", 3, TOK * D)
        hst = place("hst", 5, KT * S)
        PF = PASSES[0] * GROUP
        f_hi = place("f_hi", 3, PF * S, F32R)
        f_lo = place("f_lo", 6, PF * S, F32R)
        silu = place("silu", 9, GROUP * S)
        f32_ = place("f32_", 9.5, GROUP * S)
        y_out = place("y_out", 3, TOK * D)

        bank = [ctx.enter_context(nc.psum_tensor(f"bank{i}", [P, 2 * 512], F32)) for i in range(4)]

        raw_full = [sem(f"raw_full{i}") for i in range(RING)]
        hi_done = sem("hi_done")
        lo_done = sem("lo_done")
        chunk_used = sem("chunk_used")
        mod_full = [sem(f"mod_full{i}") for i in range(MOD_RING)]
        mod_used = sem("mod_used")
        side_done = {b: sem(f"side_done{b}") for b in (2, 3)}
        free = [sem(f"free{i}") for i in range(4)]
        par_in = sem("par_in")
        x_in = sem("x_in")
        gw_in = sem("gw_in")
        rows_in = sem("rows_in")
        nf_in = sem("nf_in")
        res_in = sem("res_in")
        out_done = sem("out_done")
        ones_set = sem("ones_set")
        dve_order = sem("dve_order")
        silu_c_done = sem("silu_c_done")
        squared = sem("squared")
        mean_done = sem("mean_done")
        root_done = sem("root_done")
        normed = sem("normed")
        turned = sem("turned")
        neg_abs_done = sem("neg_abs_done")
        exp_done = sem("exp_done")
        softplus_done = sem("softplus_done")
        conv_done = sem("conv_done")
        tanh_done = sem("tanh_done")
        ixc_done = sem("ixc_done")
        sqrt_done = sem("sqrt_done")
        lru_f32 = sem("lru_f32")
        lru_high = sem("lru_high")
        lru_low = sem("lru_low")
        sc_f32 = sem("sc_f32")
        sc_high = sem("sc_high")
        sc_low = sem("sc_low")
        pool_f32 = sem("pool_f32")
        pool_high = sem("pool_high")
        pool_low = sem("pool_low")
        h_f32 = sem("h_f32")
        h_high = sem("h_high")
        h_low = sem("h_low")
        fin_done = sem("fin_done")
        mg_high = sem("mg_high")
        mg_low = sem("mg_low")
        f_high = sem("f_high")
        f_low = sem("f_low")
        res_done = sem("res_done")
        y_done = sem("y_done")

        def plus(const, step=0, i=0):
            return const + step * i if step else const

        block = ctx.enter_context(nc.Block())

        @block.sync
        def _(sync):
            def load(slot, chunk):
                return sync.dma_start(raw[slot][:, :], w_stream[chunk, :, :]).then_inc(raw_full[slot], 16)

            for t in range(TOK):
                sync.dma_start(x_tok[:, t * D:(t + 1) * D], x[t * P:(t + 1) * P, :]).then_inc(x_in, 16)
            for c in range(RING):
                load(c, c)
            with sync.Fori(1, N_CHUNKS // RING) as r:
                for c in range(RING):
                    sync.wait_ge(lo_done, 4 * r + (c - RING + 1))
                    sync.dma_start(raw[c][:, :],
                                   w_stream[bass.ds(4 * r + c, 1), :, :].rearrange("a p c -> p (a c)"))\
                        .then_inc(raw_full[c], 16)

        @block.gpsimd
        def _(pool):
            pool.dma_start(ident[:, :], ident_in).then_inc(par_in, 16)
            pool.dma_start(par[:, :], params).then_inc(par_in, 16)
            for c in range(MOD_RING):
                pool.dma_start(mod_raw[c][:, :], m_stream[c, :, :]).then_inc(mod_full[c], 16)
            with pool.Fori(1, N_MOD // MOD_RING) as r:
                for c in range(MOD_RING):
                    pool.wait_ge(mod_used, 4 * r + (c - MOD_RING + 1))
                    pool.dma_start(mod_raw[c][:, :],
                                   m_stream[bass.ds(4 * r + c, 1), :, :].rearrange("a p c -> p (a c)"))\
                        .then_inc(mod_full[c], 16)

        @block.tensor
        def _(pe):
            def product(b, hi, lo, chunk, step, i, chunks, rhs0=0, ready=None):
                for c in range(chunks):
                    slot = (chunk + c) % RING
                    pe.wait_ge(lo_done, plus(chunk + c + 1, step, i))
                    if ready is not None:
                        pe.wait_ge(h_low, ready + c + 1)
                    for kk in range(2):
                        k = rhs0 + 2 * c + kk
                        act_hi, act_lo = hi[:, k * S:(k + 1) * S], lo[:, k * S:(k + 1) * S]
                        for m in range(GROUP):
                            acc = bank[b][:, m * S:(m + 1) * S]
                            cols = slice(kk * 512 + m * P, kk * 512 + (m + 1) * P)
                            first = c == 0 and kk == 0 and m % 2 == 0
                            last = c == chunks - 1 and kk == 1
                            nc.tensor.matmul(acc, w_hi[slot][:, cols], act_hi, start=first, stop=False,
                                             skip_group_check=True)
                            nc.tensor.matmul(acc, w_hi[slot][:, cols], act_lo, start=False, stop=False,
                                             skip_group_check=True)
                            mm = nc.tensor.matmul(acc, w_lo[slot][:, cols], act_hi, start=False, stop=last,
                                                  skip_group_check=True)
                    mm.then_inc(chunk_used, 1)

            def wide(half, hi, lo, chunk, kts):
                for k in range(kts):
                    slot = (chunk + k) % RING
                    pe.wait_ge(lo_done, chunk + k + 1)
                    for t in range(TOK):
                        b = (2 if half == 0 else 0) + t
                        cols = slice(k * S + t * P, k * S + (t + 1) * P)
                        terms = ((hi, w_hi), (hi, w_lo), (lo, w_hi))
                        for n, (act, w) in enumerate(terms):
                            for q in range(2):
                                mm = nc.tensor.matmul(bank[b][:, q * 512:(q + 1) * 512], act[:, cols],
                                                      w[slot][:, q * 512:(q + 1) * 512],
                                                      start=(k == 0 and n == 0), stop=(k == kts - 1 and n == 2))
                    mm.then_inc(chunk_used, 1)

            def bank_free(b, uses):
                if uses:
                    pe.wait_ge(free[b], uses)

            def mod_half(task, m, row):
                b, uses, _ = side_use(task)
                bank_free(b, uses)
                pe.wait_ge(mod_used, MOD_HALF * (m + 1))
                for j in range(CHUNK // P if not row else 2):
                    if row:
                        mm = nc.tensor.matmul(bank[b][:, j * 512:(j + 1) * 512], ones[:, :],
                                              mod_acc[m % 2][:, j * 512:(j + 1) * 512], start=True, stop=True)
                    else:
                        mm = nc.tensor.transpose(bank[b][:, j * P:(j + 1) * P],
                                                 mod_acc[m % 2][:, j * P:(j + 1) * P], ident[:, :])
                mm.then_inc(side_done[b], 1)

            def turn(b, src, quarter, done):
                for j in range(GROUP):
                    for t in range(TOK):
                        at = t * D + (quarter * GROUP + j) * P
                        mm = nc.tensor.transpose(bank[b][:, j * S + t * P:j * S + (t + 1) * P],
                                                 src[:, at:at + P], ident[:, :])
                mm.then_inc(done, 1)

            pe.wait_ge(par_in, 32)
            pe.wait_ge(normed, TOK)
            for q in range(4):
                b, uses, _ = side_use(f"x{q}")
                bank_free(b, uses)
                turn(b, x_tok, q, side_done[b])
            pe.wait_ge(ones_set, 1)
            for m in range(4):
                mod_half(f"m{m}", m, row=False)

            product(0, h_hi, h_lo, 0, 0, 0, G_CHUNKS, ready=0)
            product(1, h_hi, h_lo, G_CHUNKS, 0, 0, G_CHUNKS)
            for b in range(2):
                bank_free(b, 1)
                product(b, h_hi, h_lo, (2 + b) * G_CHUNKS, 0, 0, G_CHUNKS)

            pe.wait_ge(gw_in, 32)
            pe.wait_ge(conv_done, BT)
            for name, w in (("r", w_ga), ("i", w_gx)):
                for half in range(2):
                    b, uses, _ = side_use(f"{name}{half}")
                    bank_free(b, uses)
                    for j in range(GROUP):
                        t = half * GROUP + j
                        mm = nc.tensor.matmul(bank[b][:, j * S:(j + 1) * S], w[:, t * P:(t + 1) * P],
                                              xc[:, t * S:(t + 1) * S], start=True, stop=True)
                    mm.then_inc(side_done[b], 1)

            pe_acc = 2
            with pe.Fori(0, A_GROUPS // 2 - 2) as i:
                for b in range(2):
                    pe.wait_ge(free[b], plus(pe_acc, 1, i))
                    product(b, h_hi, h_lo, (4 + b) * G_CHUNKS, 2 * G_CHUNKS, i, G_CHUNKS)
            pe_acc += A_GROUPS // 2 - 2
            mod_half("m4", 4, row=True)
            mod_half("m5", 5, row=True)

            def branch(chunk0, acts, uses, ready):
                with pe.Fori(0, 4) as i:
                    pe.wait_ge(free[0], plus(uses, 1, i))
                    product(0, h_hi, h_lo, chunk0, PAIR, i, G_CHUNKS)
                    pe.wait_ge(free[1], plus(uses, 1, i))
                    pe.wait_ge(ready, 1)
                    product(1, *acts, chunk0 + G_CHUNKS, PAIR, i, OUT_CHUNKS)

            branch(LRU_OUT, (lru_hi, lru_lo), pe_acc, lru_low)
            pe_acc += 4
            mod_half("m6", 6, row=False)
            mod_half("m7", 7, row=False)

            for b in range(2):
                bank_free(b, pe_acc)
                product(b, h_hi, h_lo, POOL_IN + b * G_CHUNKS, 0, 0, G_CHUNKS)
            pe_acc += 1
            branch(SC_OUT, (sc_hi, sc_lo), pe_acc, sc_low)
            pe_acc += 4
            mod_half("m8", 8, row=False)
            mod_half("m9", 9, row=False)

            for j in range(4):
                bank_free(0, pe_acc + j)
                product(0, h_hi, h_lo, POOL_OUT + j * POOL_PAIR, 0, 0, G_CHUNKS)
                bank_free(1, pe_acc + j)
                if j == 0:
                    pe.wait_ge(pool_low, 1)
                product(1, pool_hi, pool_lo, POOL_OUT + j * POOL_PAIR + G_CHUNKS, 0, 0, 1, rhs0=2 * j)
            pe_acc += 4

            pe.wait_ge(mg_low, 4)
            for b in (2, 3):
                bank_free(b, side_use("wide_o"))
            wide(0, mg_hi, mg_lo, W_O, KT)
            for b in (0, 1):
                bank_free(b, pe_acc)
            wide(1, mg_hi, mg_lo, W_O + HALF_O, KT)
            pe_acc += 1

            pe.wait_ge(normed, 2 * TOK)
            for b in (2, 3):
                bank_free(b, side_use("wide_o") + 1)
            for q in range(4):
                if q >= 2:
                    pe.wait_ge(h_f32, G_CHUNKS + 2 * (q - 1))
                turn(2 + q % 2, xn2, q, turned)

            for p, groups in enumerate(PASSES):
                up, down = FFN[p]
                with pe.Fori(0, groups) as i:
                    for b in range(2):
                        pe.wait_ge(free[b], plus(pe_acc, 1, i))
                        product(b, h_hi, h_lo, up + b * G_CHUNKS, 2 * G_CHUNKS, i, G_CHUNKS,
                                ready=G_CHUNKS)
                pe_acc += groups
                if p == 0:
                    mod_half("m10", 10, row=True)
                    mod_half("m11", 11, row=True)
                for b in (2, 3):
                    bank_free(b, side_use(f"wide_f{p}"))
                pe.wait_ge(f_low, sum(PASSES[:p + 1]))
                wide(0, f_hi, f_lo, down, groups * GROUP)
                for b in (0, 1):
                    bank_free(b, pe_acc)
                wide(1, f_hi, f_lo, down + groups * GROUP, groups * GROUP)
                pe_acc += 1

        @block.scalar
        def _(act):
            act.dma_start(g1_row[:, :], rows[0:1, :].to_broadcast([P, D])).then_inc(rows_in, 16)
            act.dma_start(g2_row[:, :], rows[1:2, :].to_broadcast([P, D])).then_inc(rows_in, 16)
            act.dma_start(cnt[:, :], pool_cnt).then_inc(rows_in, 16)
            act.dma_start(w_ga[:, :], gate_w[0]).then_inc(gw_in, 16)
            act.dma_start(w_gx[:, :], gate_w[1]).then_inc(gw_in, 16)

            def high(chunk, step=0, i=0, n=1):
                for c in range(chunk, chunk + n):
                    if c >= N_CHUNKS:
                        return
                    act.wait_ge(raw_full[c % RING], plus(16 * (c // RING + 1), 16 * step // RING, i))
                    if c >= RING:
                        act.wait_ge(chunk_used, plus(c - RING + 1, step, i))
                    nc.scalar.activation(w_hi[c % RING][:, :], raw[c % RING][:, :], ACT.Copy).then_inc(hi_done, 1)

            act.wait_ge(par_in, 32)
            nc.scalar.activation(silu_c[:, :], par[:, P_C:P_C + KT], ACT.Silu).then_inc(silu_c_done, 1)
            act.wait_ge(x_in, 32)

            def squares(junk, src, to, norm, t):
                if norm * TOK + t:
                    act.wait_ge(squared, norm * TOK + t)
                nc.scalar.activation(junk, src[:, t * D:(t + 1) * D], ACT.Square,
                                     accum_out=stat[:, to + t:to + t + 1]).then_inc(squared, 1)

            for t in range(TOK):
                squares(sq_junk[:, :], x_tok, 0, 0, t)
            act.wait_ge(mean_done, 1)
            nc.scalar.activation(stat[:, 4:6], stat[:, 2:4], ACT.Sqrt).then_inc(root_done, 1)
            act.wait_ge(neg_abs_done, 1)
            nc.scalar.activation(sp[:, BT:2 * BT], sp[:, 0:BT], ACT.Exp).then_inc(exp_done, 1)

            for q in range(4):
                b, _, done = side_use(f"x{q}")
                act.wait_ge(side_done[b], done)
                nc.scalar.activation(xn[:, q * CHUNK:(q + 1) * CHUNK], bank[b][:, :], ACT.Copy).then_inc(free[b], 1)
            high(0, n=RING)

            def h_high_parts(src, first):
                for q in range(G_CHUNKS):
                    act.wait_ge(h_f32, first + q + 1)
                    nc.scalar.activation(h_hi[:, q * 512:(q + 1) * 512], src[:, q * 512:(q + 1) * 512],
                                         ACT.Copy).then_inc(h_high, 1)

            h_high_parts(xn, 0)

            def take(dst, g, func=ACT.Copy):
                act.wait_ge(chunk_used, (g + 1) * G_CHUNKS)
                nc.scalar.activation(dst[:, (g % 2) * CHUNK:(g % 2 + 1) * CHUNK], bank[g % 2][:, :], func)\
                    .then_inc(free[g % 2], 1)

            def r_or_i(name, dst, bias):
                for half in range(2):
                    b, _, done = side_use(f"{name}{half}")
                    act.wait_ge(side_done[b], done)
                    for j in range(GROUP):
                        t = half * GROUP + j
                        ins = nc.scalar.activation(dst[:, t * S:(t + 1) * S], bank[b][:, j * S:(j + 1) * S],
                                                   ACT.Sigmoid, bias=par[:, bias + t:bias + t + 1])
                    ins.then_inc(free[b], 1)

            targets = [lx, lg, sb_, sc_]
            for g in range(A_GROUPS):
                high(g * G_CHUNKS + RING, n=G_CHUNKS)
                if g < 8:
                    take(targets[g // 2], g, ACT.Gelu_apprx_tanh if g // 2 == 1 else ACT.Copy)
                if g == 3:
                    r_or_i("r", lr, P_BA)
                    r_or_i("i", li, P_BX)
                    act.wait_ge(softplus_done, 1)
                    b, uses, _ = side_use("r1")
                    act.wait_ge(free[b], uses + 1)
                    for t in range(BT):
                        ins = nc.scalar.activation(lr[:, t * S:(t + 1) * S], lr[:, t * S:(t + 1) * S], ACT.Tanh,
                                                   scale=sp[:, 7 * BT + t:7 * BT + t + 1])
                    ins.then_inc(tanh_done, 1)
                    act.wait_ge(tanh_done, 1)
                if g == 4:
                    act.wait_ge(ixc_done, 1)
                    nc.scalar.activation(xc[:, :], lr[:, :], ACT.Sqrt).then_inc(sqrt_done, 1)
                if g == 7:
                    act.wait_ge(lru_f32, 1)
                    nc.scalar.activation(lru_hi[:, :], lg[:, :], ACT.Copy).then_inc(lru_high, 1)

            def sigmoid_gates(chunk_end, step, i, uses):
                act.wait_ge(chunk_used, plus(chunk_end, step, i))
                act.wait_ge(free[1], plus(uses, 1 if step else 0, i))
                nc.scalar.activation(gate[:, :], bank[0][:, :], ACT.Sigmoid).then_inc(free[0], 1)

            def gates(chunk0, uses):
                with act.Fori(0, 4) as i:
                    high(chunk0 + RING, PAIR, i, G_CHUNKS)
                    sigmoid_gates(chunk0 + G_CHUNKS, PAIR, i, uses)
                    high(chunk0 + RING + G_CHUNKS, PAIR, i, OUT_CHUNKS)

            gates(LRU_OUT, A_GROUPS // 2)
            uses = A_GROUPS // 2 + 4
            act.wait_ge(sc_f32, 1)
            nc.scalar.activation(sc_hi[:, :], sv[:, :], ACT.Copy).then_inc(sc_high, 1)
            for b in range(2):
                high(POOL_IN + b * G_CHUNKS + RING, n=G_CHUNKS)
                act.wait_ge(chunk_used, POOL_IN + (b + 1) * G_CHUNKS)
                nc.scalar.activation(pu[:, b * CHUNK:(b + 1) * CHUNK], bank[b][:, :], ACT.Copy).then_inc(free[b], 1)
            uses += 1
            gates(SC_OUT, uses)
            uses += 4
            act.wait_ge(pool_f32, 1)
            nc.scalar.activation(pool_hi[:, :], pa[:, :], ACT.Copy).then_inc(pool_high, 1)
            for j in range(4):
                chunk = POOL_OUT + j * POOL_PAIR
                high(chunk + RING, n=G_CHUNKS)
                sigmoid_gates(chunk + G_CHUNKS, 0, 0, uses + j)
                high(chunk + RING + G_CHUNKS)
                act.wait_ge(fin_done, j + 1)
                nc.scalar.activation(mg_hi[:, j * CHUNK:(j + 1) * CHUNK], merged[:, j * CHUNK:(j + 1) * CHUNK],
                                     ACT.Copy).then_inc(mg_high, 1)
            uses += 4
            for t in range(TOK):
                act.dma_start(res[:, t * D:(t + 1) * D], x[t * P:(t + 1) * P, :]).then_inc(res_in, 16)
            act.dma_start(nf_row[:, :], rows[2:3, :].to_broadcast([P, D])).then_inc(nf_in, 16)
            high(W_O + RING, n=2 * HALF_O)
            for t in range(TOK):
                act.wait_ge(res_done, t + 1)
                squares(xn2[:, t * D:(t + 1) * D], res, 6, 1, t)
            act.wait_ge(mean_done, 2)
            nc.scalar.activation(stat[:, 10:12], stat[:, 8:10], ACT.Sqrt).then_inc(root_done, 1)
            h_high_parts(hst, G_CHUNKS)
            uses += 1

            for p, groups in enumerate(PASSES):
                up, down = FFN[p]
                before = sum(PASSES[:p])
                with act.Fori(0, groups) as i:
                    high(up + RING, 2 * G_CHUNKS, i, G_CHUNKS)
                    act.wait_ge(chunk_used, plus(up + G_CHUNKS, 2 * G_CHUNKS, i))
                    act.wait_ge(free[1], plus(uses, 1, i))
                    nc.scalar.activation(silu[:, :], bank[0][:, :], ACT.Silu).then_inc(free[0], 1)
                    high(up + RING + G_CHUNKS, 2 * G_CHUNKS, i, G_CHUNKS)
                    act.wait_ge(free[1], plus(uses + 1, 1, i))
                    nc.scalar.activation(f_hi[:, bass.ds(i * CHUNK, CHUNK)], f32_[:, :], ACT.Copy)\
                        .then_inc(f_high, 1)
                uses += groups + 1
                high(down + RING, n=2 * groups * GROUP)

            for t in range(TOK):
                act.wait_ge(res_done, TOK + t + 1)
                squares(y_out[:, t * D:(t + 1) * D], res, 0, 2, t)
                act.wait_ge(mean_done, 3 + t)
                nc.scalar.activation(stat[:, 4 + t:5 + t], stat[:, 2 + t:3 + t], ACT.Sqrt).then_inc(root_done, 1)
            for t in range(TOK):
                act.wait_ge(y_done, t + 1)
                act.dma_start(out[t * P:(t + 1) * P, :], y_out[:, t * D:(t + 1) * D]).then_inc(out_done, 16)
            act.wait_ge(out_done, 16 * TOK)

        @block.vector
        def _(dve):
            def step(ins, done=dve_order):
                ins.then_inc(done, 1)
                stood[done.name] = stood.get(done.name, 0) + 1
                dve.wait_ge(done, stood[done.name])

            stood = {}
            V = nc.vector

            def low(chunk, stride=0, i=0, n=1):
                for c in range(chunk, chunk + n):
                    if c >= N_CHUNKS:
                        return
                    dve.wait_ge(hi_done, plus(c + 1, stride, i))
                    V.tensor_tensor(w_lo[c % RING][:, :], raw[c % RING][:, :], w_hi[c % RING][:, :].bitcast(F32),
                                    ALU.subtract).then_inc(lo_done, 1)

            def half_reduced(m):
                b, _, done = side_use(f"m{m}")
                dve.wait_ge(side_done[b], done)

            def mod(m, n=1):
                for c in range(m, m + n):
                    k, acc = c % MOD_HALF, mod_acc[(c // MOD_HALF) % 2]
                    dve.wait_ge(mod_full[c % MOD_RING], 16 * (c // MOD_RING + 1))
                    if k == 0:
                        if c >= 2 * MOD_HALF:
                            half_reduced(c // MOD_HALF - 2)
                        else:
                            dve.wait_ge(silu_c_done, 1)
                        V.tensor_scalar(acc[:, :], mod_raw[c % MOD_RING][:, :], silu_c[:, 0:1], None,
                                        ALU.mult).then_inc(mod_used, 1)
                    else:
                        dve.wait_ge(mod_used, c)
                        V.scalar_tensor_tensor(out=acc[:, :], in0=mod_raw[c % MOD_RING][:, :],
                                               scalar=silu_c[:, k:k + 1], in1=acc[:, :],
                                               op0=ALU.mult, op1=ALU.add).then_inc(mod_used, 1)

            def sums(task, dst, at):
                b, uses, done = side_use(task)
                dve.wait_ge(side_done[b], done)
                V.tensor_reduce(dst[:, at:at + CHUNK // P], bank[b][:, :].rearrange("p (j k) -> p j k", k=P),
                                AX.X, ALU.add).then_inc(free[b], 1)
                dve.wait_ge(free[b], uses + 1)

            def row_sums(task, dst, half):
                b, uses, done = side_use(task)
                dve.wait_ge(side_done[b], done)
                cols = slice(half * CHUNK, (half + 1) * CHUNK)
                V.tensor_tensor(dst[:, cols], bank[b][:, :], dst[:, cols], ALU.add).then_inc(free[b], 1)
                dve.wait_ge(free[b], uses + 1)

            def affine(sc_at, sh_at, b_sc, b_sh, norm, to):
                step(V.tensor_tensor(modc[:, sc_at:sc_at + KT], modc[:, sc_at:sc_at + KT],
                                     par[:, P_BMOD + b_sc * KT:P_BMOD + (b_sc + 1) * KT], ALU.add))
                step(V.scalar_tensor_tensor(out=aff[:, to:to + KT], in0=modc[:, sc_at:sc_at + KT], scalar=1.0,
                                            in1=par[:, norm:norm + KT], op0=ALU.add, op1=ALU.mult))
                step(V.tensor_tensor(aff[:, to + KT:to + 2 * KT], modc[:, sh_at:sh_at + KT],
                                     par[:, P_BMOD + b_sh * KT:P_BMOD + (b_sh + 1) * KT], ALU.add))

            V.memset(ones[:, :], 1.0).then_inc(ones_set, 1)
            dve.wait_ge(ones_set, 1)
            dve.wait_ge(par_in, 32)
            lam = par[:, P_LAM:P_LAM + BT]

            def spc(i):
                return sp[:, i * BT:(i + 1) * BT]

            step(V.tensor_scalar(spc(2), lam, -1.0, 0.0, ALU.mult, ALU.max))
            step(V.scalar_tensor_tensor(out=spc(0), in0=spc(2), scalar=-2.0, in1=lam, op0=ALU.mult,
                                        op1=ALU.subtract), neg_abs_done)
            dve.wait_ge(squared, 2)
            step(V.tensor_scalar(stat[:, 2:4], stat[:, 0:2], 1.0 / D, EPS, ALU.mult, ALU.add), mean_done)
            dve.wait_ge(root_done, 1)
            step(V.reciprocal(stat[:, 4:6], stat[:, 4:6]))
            for t in range(TOK):
                step(V.tensor_scalar(x_tok[:, t * D:(t + 1) * D], x_tok[:, t * D:(t + 1) * D],
                                     stat[:, 4 + t:5 + t], None, ALU.mult), normed)
            mod(0, MOD_HALF)
            dve.wait_ge(exp_done, 1)
            step(V.tensor_scalar(spc(3), spc(1), 2.0, None, ALU.add))
            step(V.reciprocal(spc(3), spc(3)))
            step(V.tensor_tensor(spc(3), spc(3), spc(1), ALU.mult))
            step(V.tensor_tensor(spc(4), spc(3), spc(3), ALU.mult))
            step(V.memset(spc(5), 1.0 / 17))
            for n in range(15, 0, -2):
                step(V.tensor_tensor(spc(5), spc(5), spc(4), ALU.mult))
                step(V.tensor_scalar(spc(5), spc(5), 1.0 / n, None, ALU.add))
            step(V.tensor_tensor(spc(5), spc(5), spc(3), ALU.mult))
            step(V.scalar_tensor_tensor(out=spc(6), in0=spc(5), scalar=2.0, in1=spc(2), op0=ALU.mult, op1=ALU.add))
            step(V.tensor_scalar(spc(7), spc(6), 4.0, None, ALU.mult), softplus_done)
            mod(MOD_HALF, 3 * MOD_HALF)
            low(0, n=RING)
            for m in range(4):
                sums(f"m{m}", modc, m * CHUNK // P)
            affine(0, KT, 1, 0, P_NMIX, 0)

            def modulate(src_of, dst, at, first):
                def f32_pair(q):
                    for k in (2 * q, 2 * q + 1):
                        ins = V.tensor_scalar(dst[:, k * S:(k + 1) * S], src_of(k), aff[:, at + k:at + k + 1],
                                              aff[:, at + KT + k:at + KT + k + 1], ALU.mult, ALU.add)
                    ins.then_inc(h_f32, 1)

                f32_pair(0)
                for q in range(G_CHUNKS):
                    if q + 1 < G_CHUNKS:
                        f32_pair(q + 1)
                    dve.wait_ge(h_high, first + q + 1)
                    V.tensor_tensor(h_lo[:, q * 512:(q + 1) * 512], dst[:, q * 512:(q + 1) * 512],
                                    h_hi[:, q * 512:(q + 1) * 512].bitcast(F32), ALU.subtract).then_inc(h_low, 1)

            for q in (2, 3):
                b, uses, _ = side_use(f"x{q}")
                dve.wait_ge(free[b], uses + 1)
            modulate(lambda k: xn[:, k * S:(k + 1) * S], xn, 0, 0)

            def three_d(t):
                return t[:, :].rearrange("p (j s) -> p j s", s=S)

            def conv(dst, src, tiles, taps, width, bias=None, done=dve_order):
                for t in tiles:
                    o, u = t * S, (t + 1) * S
                    w = taps + (width - 1) * BT + t
                    if bias is None:
                        step(V.tensor_scalar(dst[:, o:u], src[:, o:u], par[:, w:w + 1], None, ALU.mult))
                    else:
                        step(V.tensor_scalar(dst[:, o:u], src[:, o:u], par[:, w:w + 1],
                                             par[:, bias + t:bias + t + 1], ALU.mult, ALU.add))
                    for back in range(1, width):
                        w = taps + (width - 1 - back) * BT + t
                        step(V.scalar_tensor_tensor(out=dst[:, o + back:u], in0=src[:, o:u - back],
                                                    scalar=par[:, w:w + 1], in1=dst[:, o + back:u],
                                                    op0=ALU.mult, op1=ALU.add),
                             done if back == width - 1 else dve_order)

            for g in range(A_GROUPS):
                for c in range(G_CHUNKS):
                    low(g * G_CHUNKS + RING + c)
                    if g < 8 and c % 2 == 1:
                        mod(64 + 4 * g + c // 2)
                    if g == 4 and c == 2:
                        dve.wait_ge(tanh_done, 1)
                        step(V.tensor_tensor(li[:, :], li[:, :], xc[:, :], ALU.mult), ixc_done)
                    if g == 4 and c == 4:
                        step(V.tensor_scalar(lx[:, :], lr[:, :], 1.0, None, ALU.add))
                        step(V.reciprocal(lx[:, :], lx[:, :]))
                    if g == 5 and c == 0:
                        dve.wait_ge(sqrt_done, 1)
                        step(V.scalar_tensor_tensor(out=xc[:, :], in0=xc[:, :], scalar=2.0, in1=lx[:, :],
                                                    op0=ALU.mult, op1=ALU.mult))
                        step(V.memset(three_d(xc)[:, :, 0:1], 1.0))
                    if g == 5 and c == 2:
                        step(V.tensor_tensor(li[:, :], li[:, :], xc[:, :], ALU.mult))
                    if g == 5 and c == 4:
                        step(V.tensor_scalar(lr[:, :], lr[:, :], -1.0, 1.0, ALU.mult, ALU.add))
                        step(V.tensor_tensor(lr[:, :], lr[:, :], lx[:, :], ALU.mult))
                        step(V.memset(three_d(lr)[:, :, 0:1], 0.0))
                    if g == 6 and c == 0:
                        step(V.tensor_tensor_scan(lx[:, :], lr[:, :], li[:, :], 0.0, ALU.mult, ALU.add))
                    if g == 6 and c == 4:
                        step(V.tensor_tensor(lg[:, :], lg[:, :], lx[:, :], ALU.mult), lru_f32)
                if g < 2:
                    dve.wait_ge(free[g], 1)
                    conv(xc, lx, range(4 * g, 4 * g + 4), P_CONVW, 4, P_CONVB, conv_done)
                if g >= 8:
                    b = g % 2
                    cols = slice(b * CHUNK, (b + 1) * CHUNK)
                    dve.wait_ge(chunk_used, (g + 1) * G_CHUNKS)
                    V.tensor_tensor(sc_[:, cols], bank[b][:, :], sc_[:, cols], ALU.mult).then_inc(free[b], 1)
                if g == 8:
                    dve.wait_ge(lru_high, 1)
                    step(V.tensor_tensor(lru_lo[:, :], lg[:, :], lru_hi[:, :].bitcast(F32), ALU.subtract), lru_low)
            dve.wait_ge(rows_in, 48)
            row_sums("m4", g1_row, 0)
            row_sums("m5", g1_row, 1)

            def merge(j, uses, branch_no, chunk_end):
                dst = merged[:, j * CHUNK:(j + 1) * CHUNK]
                dve.wait_ge(free[0], uses + j + 1)
                dve.wait_ge(chunk_used, chunk_end)
                if branch_no == 0:
                    V.tensor_tensor(dst, bank[1][:, :], gate[:, :], ALU.mult).then_inc(free[1], 1)
                    return
                if branch_no == 1:
                    V.tensor_tensor(term[:, :], bank[1][:, :], gate[:, :], ALU.mult).then_inc(free[1], 1)
                else:
                    for m in range(GROUP):
                        cols = slice(m * S, (m + 1) * S)
                        at = P_PSCALE + j * GROUP + m
                        ins = V.scalar_tensor_tensor(out=term[:, cols], in0=bank[1][:, cols],
                                                     scalar=par[:, at:at + 1], in1=gate[:, cols],
                                                     op0=ALU.mult, op1=ALU.mult)
                    ins.then_inc(free[1], 1)
                dve.wait_ge(free[1], uses + j + 1)
                step(V.tensor_tensor(dst, dst, term[:, :], ALU.add), fin_done if branch_no == 2 else dve_order)

            uses = A_GROUPS // 2
            for j in range(4):
                for c in range(PAIR):
                    low(LRU_OUT + j * PAIR + RING + c)
                    if c < 8:
                        mod(96 + 8 * j + c)
                    if c in (9, 10):
                        conv(sv, sc_, (2 * j + c - 9,), P_SCW, 3)
                merge(j, uses, 0, LRU_OUT + (j + 1) * PAIR)
            uses += 4
            sums("m6", modc, 2 * KT)
            sums("m7", modc, 2 * KT + CHUNK // P)
            step(V.tensor_tensor(sv[:, :], sv[:, :], sb_[:, :], ALU.mult), sc_f32)
            low(POOL_IN + RING, n=G_CHUNKS)
            dve.wait_ge(sc_high, 1)
            step(V.tensor_tensor(sc_lo[:, :], sv[:, :], sc_hi[:, :].bitcast(F32), ALU.subtract), sc_low)
            low(POOL_IN + G_CHUNKS + RING, n=G_CHUNKS)
            uses += 1

            def pool_means():
                tiles = BT // 4
                for g, window in enumerate(POOL_WINDOWS):
                    cols = slice(g * tiles * S, (g + 1) * tiles * S)
                    src, w = pu, 1
                    for dst in (pa, pb, pa, pb)[:g + 1]:
                        s3 = src[:, cols].rearrange("p (j s) -> p j s", s=S)
                        d3 = dst[:, cols].rearrange("p (j s) -> p j s", s=S)
                        step(V.tensor_tensor(d3[:, :, w:], s3[:, :, w:], s3[:, :, :S - w], ALU.add))
                        step(V.tensor_copy(d3[:, :, 0:w], s3[:, :, 0:w]))
                        src, w = dst, 2 * w
                    dst = pa
                    s3 = src[:, cols].rearrange("p (j s) -> p j s", s=S)
                    at = sum(POOL_WINDOWS[:g])
                    for j in range(tiles):
                        step(V.tensor_tensor(s3[:, j, 0:window], s3[:, j, 0:window], cnt[:, at:at + window],
                                             ALU.mult))
                    step(V.scalar_tensor_tensor(out=dst[:, cols], in0=src[:, cols], scalar=1.0 / window,
                                                in1=pu[:, cols], op0=ALU.mult, op1=ALU.subtract),
                         pool_f32 if g == 3 else dve_order)
                    yield

            dve.wait_ge(free[0], uses)
            dve.wait_ge(free[1], uses)
            pooling = pool_means()
            for j in range(4):
                for c in range(PAIR):
                    low(SC_OUT + j * PAIR + RING + c)
                    if c < 8:
                        mod(128 + 8 * j + c)
                    if c == 9:
                        next(pooling)
                merge(j, uses, 1, SC_OUT + (j + 1) * PAIR)
            uses += 4
            sums("m8", modc, 3 * KT)
            sums("m9", modc, 3 * KT + CHUNK // P)
            affine(3 * KT, 2 * KT, 4, 3, P_NFFN, 2 * KT)

            low(POOL_OUT + RING)
            dve.wait_ge(pool_high, 1)
            step(V.tensor_tensor(pool_lo[:, :], pa[:, :], pool_hi[:, :].bitcast(F32), ALU.subtract), pool_low)
            for j in range(4):
                low(POOL_OUT + j * POOL_PAIR + RING + (j == 0), n=POOL_PAIR - (j == 0))
                merge(j, uses, 2, POOL_OUT + (j + 1) * POOL_PAIR)
                dve.wait_ge(mg_high, j + 1)
                V.tensor_tensor(mg_lo[:, j * CHUNK:(j + 1) * CHUNK], merged[:, j * CHUNK:(j + 1) * CHUNK],
                                mg_hi[:, j * CHUNK:(j + 1) * CHUNK].bitcast(F32), ALU.subtract).then_inc(mg_low, 1)
            uses += 4

            def add_half(half, g_row, side, main, chunk_end, done):
                dve.wait_ge(chunk_used, chunk_end)
                for t in range(TOK):
                    b = (2 if half == 0 else 0) + t
                    n = side if half == 0 else main
                    cols = slice(half * CHUNK, (half + 1) * CHUNK)
                    tcols = slice(t * D + half * CHUNK, t * D + (half + 1) * CHUNK)
                    V.tensor_tensor(mod_acc[t][:, :], bank[b][:, :], g_row[:, cols], ALU.mult).then_inc(free[b], 1)
                    dve.wait_ge(free[b], n + 1)
                    step(V.tensor_tensor(res[:, tcols], res[:, tcols], mod_acc[t][:, :], ALU.add),
                         done)

            half_reduced(8)
            half_reduced(9)
            low(W_O + RING, n=HALF_O)
            dve.wait_ge(res_in, 32)
            add_half(0, g1_row, side_use("wide_o"), uses, W_O + HALF_O, dve_order)
            low(W_O + HALF_O + RING, n=HALF_O)
            add_half(1, g1_row, side_use("wide_o"), uses, W_O + 2 * HALF_O, res_done)
            uses += 1

            dve.wait_ge(squared, 4)
            step(V.tensor_scalar(stat[:, 8:10], stat[:, 6:8], 1.0 / D, EPS, ALU.mult, ALU.add), mean_done)
            dve.wait_ge(root_done, 2)
            step(V.reciprocal(stat[:, 10:12], stat[:, 10:12]))
            for t in range(TOK):
                step(V.tensor_scalar(xn2[:, t * D:(t + 1) * D], res[:, t * D:(t + 1) * D],
                                     stat[:, 10 + t:11 + t], None, ALU.mult), normed)

            def turned_tile(k):
                if k % GROUP == 0:
                    dve.wait_ge(turned, k // GROUP + 1)
                return bank[2 + k // GROUP % 2][:, (k % GROUP) * S:(k % GROUP + 1) * S]

            def modulate2():
                at = 2 * KT
                for q in range(G_CHUNKS):
                    for k in (2 * q, 2 * q + 1):
                        ins = V.tensor_scalar(hst[:, k * S:(k + 1) * S], turned_tile(k), aff[:, at + k:at + k + 1],
                                              aff[:, at + KT + k:at + KT + k + 1], ALU.mult, ALU.add)
                    ins.then_inc(h_f32, 1)
                    if q:
                        low_h(q - 1)
                low_h(G_CHUNKS - 1)

            def low_h(q):
                dve.wait_ge(h_high, G_CHUNKS + q + 1)
                V.tensor_tensor(h_lo[:, q * 512:(q + 1) * 512], hst[:, q * 512:(q + 1) * 512],
                                h_hi[:, q * 512:(q + 1) * 512].bitcast(F32), ALU.subtract).then_inc(h_low, 1)

            modulate2()

            for p, groups in enumerate(PASSES):
                up, down = FFN[p]
                before = sum(PASSES[:p])

                def hidden(i, mods):
                    for c in range(2 * G_CHUNKS):
                        low(up + RING + c, 2 * G_CHUNKS, i)
                        if mods and c % 2:
                            mod(160 + 8 * i + c // 2)
                    dve.wait_ge(free[0], plus(uses + 1, 1, i))
                    dve.wait_ge(chunk_used, plus(up + 2 * G_CHUNKS, 2 * G_CHUNKS, i))
                    V.tensor_tensor(f32_[:, :], bank[1][:, :], silu[:, :], ALU.mult).then_inc(free[1], 1)
                    dve.wait_ge(f_high, plus(before + 1, 1, i))
                    hid = f_hi[:, bass.ds(i * CHUNK, CHUNK)]
                    V.tensor_tensor(f_lo[:, bass.ds(i * CHUNK, CHUNK)], f32_[:, :], hid.bitcast(F32), ALU.subtract)\
                        .then_inc(f_low, 1)

                first = 0
                if p == 0:
                    first = 4
                    for i in range(first):
                        hidden(i, True)
                with dve.Fori(first, groups) as i:
                    hidden(i, False)
                uses += groups
                if p == 0:
                    row_sums("m10", g2_row, 0)
                    row_sums("m11", g2_row, 1)
                low(down + RING, n=groups * GROUP)
                add_half(0, g2_row, side_use(f"wide_f{p}"), uses, down + groups * GROUP, dve_order)
                low(down + groups * GROUP + RING, n=groups * GROUP)
                add_half(1, g2_row, side_use(f"wide_f{p}"), uses, down + 2 * groups * GROUP,
                         res_done if p else dve_order)
                uses += 1

            dve.wait_ge(nf_in, 16)
            for t in range(TOK):
                dve.wait_ge(squared, 2 * TOK + t + 1)
                step(V.tensor_scalar(stat[:, 2 + t:3 + t], stat[:, t:t + 1], 1.0 / D, EPS, ALU.mult, ALU.add),
                     mean_done)
                dve.wait_ge(root_done, 3 + t)
                step(V.reciprocal(stat[:, 4 + t:5 + t], stat[:, 4 + t:5 + t]))
                step(V.scalar_tensor_tensor(out=y_out[:, t * D:(t + 1) * D], in0=res[:, t * D:(t + 1) * D],
                                            scalar=stat[:, 4 + t:5 + t], in1=nf_row[:, :],
                                            op0=ALU.mult, op1=ALU.mult), y_done)


_WEIGHTS = ["w_in", "lru_w_out", "sc_w_out", "pool_w", "w_o", "ffn_w1", "ffn_w3", "ffn_w2"]


def _group(np, w, col):
    k = w.shape[0] // (2 * P)
    return w[:, col:col + 512].reshape(k, 2, P, 512).transpose(0, 2, 1, 3).reshape(k, P, CHUNK)


def _half(np, w, half):
    return w[:, half * CHUNK:(half + 1) * CHUNK].reshape(-1, P, CHUNK)


def _weight_stream(np, w):
    w_in, proj = w["w_in"], 2 * W_LRU + 4 * W_LRU
    parts = [_group(np, w_in, g * 512) for g in range(A_GROUPS)]
    for j in range(4):
        parts += [_group(np, w_in, proj + j * 512), _group(np, w["lru_w_out"], j * 512)]
    parts += [_group(np, w_in, (A_GROUPS + g) * 512) for g in range(2)]
    for j in range(4):
        parts += [_group(np, w_in, proj + D + j * 512), _group(np, w["sc_w_out"], j * 512)]
    for j in range(4):
        parts += [_group(np, w_in, proj + 2 * D + j * 512), _group(np, w["pool_w"][j], 0)]
    parts += [_half(np, w["w_o"], h) for h in range(2)]
    first = 0
    for groups in PASSES:
        for g in range(first, first + groups):
            parts += [_group(np, w["ffn_w1"], g * 512), _group(np, w["ffn_w3"], g * 512)]
        parts += [_half(np, w["ffn_w2"][first * 512:(first + groups) * 512], h) for h in range(2)]
        first += groups
    return np.concatenate(parts)


def kernel(**inputs):
    import numpy as np
    import concourse.bacc as bacc
    from concourse.bass_utils import run_bass_kernel_spmd

    a = {k: np.asarray(v) for k, v in inputs.items()}
    w_stream = _weight_stream(np, {k: a[k][0] for k in _WEIGHTS})
    assert w_stream.shape == (N_CHUNKS, P, CHUNK)
    halves = a["w_mod"][0].reshape(KT, P, 2 * len(MOD_ORDER), CHUNK).transpose(2, 0, 1, 3)
    m_stream = np.concatenate([halves[2 * v + h] for v in MOD_ORDER for h in range(2)])

    def cols(v):
        return v.reshape(-1, P).T

    params = np.ascontiguousarray(np.concatenate([
        cols(a["b_mod"]), cols(a["norm_mix"]), cols(a["norm_ffn"]), cols(a["pool_scale"]), cols(a["lru_conv_w"]),
        cols(a["lru_conv_b"]), cols(a["lru_b_a"]), cols(a["lru_b_x"]), cols(a["lru_lambda"]),
        cols(a["sc_conv_w"]), cols(a["c"])], axis=1))
    assert params.shape == (P, N_PARAM)
    gate_w = np.zeros((2, P, BT, P), np.float32)
    for n, name in enumerate(("lru_w_a", "lru_w_x")):
        for head in range(2 * BT):
            o = (head % 2) * 64
            gate_w[n, o:o + 64, head // 2, o:o + 64] = a[name][0, head]
    b_mod = a["b_mod"].reshape(-1, D)
    rows = np.ascontiguousarray(np.stack([b_mod[2], b_mod[5], a["norm_final"]]))
    pool_cnt = np.tile(np.concatenate([w / np.arange(1, w + 1) for w in POOL_WINDOWS]).astype(np.float32), (P, 1))
    arrays = {
        "x": np.ascontiguousarray(a["x"][0]), "params": params, "gate_w": gate_w.reshape(2, P, BT * P),
        "rows": rows, "pool_cnt": pool_cnt, "w_stream": w_stream, "m_stream": m_stream,
        "ident": np.eye(P, dtype=np.float32),
    }
    nc = bacc.Bacc("TRN2", target_bir_lowering=False, num_devices=1)
    args = [nc.dram_tensor(f"in_{k}", v.shape, F32, kind="ExternalInput").ap() for k, v in arrays.items()]
    out = nc.dram_tensor("out_y", (S, D), F32, kind="ExternalOutput").ap()
    trunk_kernel(nc, *args, out)
    result = run_bass_kernel_spmd(nc, [{f"in_{k}": v for k, v in arrays.items()}], core_ids=[0])
    return result.results[0]["out_y"].reshape(1, S, D)
```

```python
from contextlib import ExitStack

import concourse.bass as bass
from concourse import mybir

F32 = mybir.dt.float32
F32R = mybir.dt.float32r
ALU = mybir.AluOpType
ACT = mybir.ActivationFunctionType
AX = mybir.AxisListType

P = 128
D = 2048
S = 256
FF = 5632
EPS = 1e-6
KT = D // P
TOK = S // P
W_LRU = 1024
BT = W_LRU // P
CHUNK = 1024
GROUP = 4
RING = 4
MOD_RING = 4
POOL_WINDOWS = (2, 4, 8, 16)

G_CHUNKS = KT // 2
OUT_CHUNKS = BT // 2
A_GROUPS = 10
OPENING = 3
PROJ = OPENING * G_CHUNKS
LRU_OUT = PROJ + (A_GROUPS - 2) * G_CHUNKS
PAIR = G_CHUNKS + OUT_CHUNKS
POOL_IN = LRU_OUT + 4 * PAIR
SC_OUT = POOL_IN + G_CHUNKS
POOL_OUT = SC_OUT + 4 * PAIR
POOL_PAIR = G_CHUNKS + 1
W_O = POOL_OUT + 4 * POOL_PAIR
HALF_O = KT
PASSES = (6, 5)
FFN = []
_n = W_O + 2 * HALF_O
for _g in PASSES:
    FFN.append((_n, _n + _g * 2 * G_CHUNKS))
    _n = FFN[-1][1] + 2 * GROUP * _g
N_CHUNKS = _n
MOD_HALF = KT
MOD_ORDER = (1, 0, 2, 3, 4, 5)
N_MOD = 2 * MOD_HALF * len(MOD_ORDER)
OPENING_MOD = 4 * MOD_HALF

P_BMOD = 0
P_NMIX = 96
P_NFFN = 112
P_PSCALE = 128
P_CONVW = 144
P_CONVB = 176
P_BA = 184
P_BX = 192
P_LAM = 200
P_SCW = 208
P_C = 232
P_B1 = 248
N_PARAM = 280

SIDE = [("x0", 2), ("x1", 3), ("s0", 2), ("x2", 3), ("x3", 2), ("pool", 3)] + [(f"s{q}", 2) for q in range(1, G_CHUNKS)] + [
    ("r0", 2), ("r1", 3), ("i0", 2), ("i1", 3), ("m4", 2), ("m5", 3), ("m6", 2), ("m7", 3), ("m8", 2), ("m9", 3),
    ("wide_o", 2), ("wide_o", 3), ("turn2", 2), ("turn3", 3), ("m10", 2), ("m11", 3), ("wide_f0", 2),
    ("wide_f0", 3), ("wide_f1", 2), ("wide_f1", 3)]


def side_use(task, bank=None):
    bank = bank or dict(SIDE)[task]
    before = [t for t, b in SIDE[:SIDE.index((task, bank))] if b == bank]
    return bank, len(before), 1 + sum(not t.startswith(("wide", "pool", "turn")) for t in before)


def trunk_kernel(nc, x, params, gate_w, rows, pool_cnt, w_stream, m_stream, ident_in, out):
    with ExitStack() as ctx:

        def sb(name, cols, dt=F32, at=None):
            return ctx.enter_context(nc.sbuf_tensor(name, [P, cols], dt)) if at is None else \
                nc.alloc_sbuf_tensor_at(name, [P, cols], dt, offset=at)

        def sem(name):
            return ctx.enter_context(nc.semaphore(name))

        raw = [sb(f"raw{i}", CHUNK) for i in range(RING)]
        w_hi = [sb(f"w_hi{i}", CHUNK, F32R) for i in range(RING)]
        w_lo = [sb(f"w_lo{i}", CHUNK, F32R) for i in range(RING)]
        mod_raw = [sb(f"mod_raw{i}", CHUNK) for i in range(MOD_RING)]
        h_hi = sb("h_hi", KT * S, F32R)
        h_lo = sb("h_lo", KT * S, F32R)
        mod_acc = [sb(f"mod_acc{i}", CHUNK) for i in range(2)]
        g1_row = sb("g1_row", D)
        g2_row = sb("g2_row", D)
        par = sb("par", N_PARAM)
        modc = sb("modc", 4 * KT)
        aff = sb("aff", 3 * KT)
        silu_c = sb("silu_c", KT)
        sp = sb("sp", 8 * BT)
        stat = sb("stat", 24)
        eps = sb("eps", 1)
        ident = sb("ident", P)
        ones = sb("ones", P)
        cnt = sb("cnt", sum(POOL_WINDOWS))

        SLOT = D * 4
        r0 = -(-nc.sbuf_base // 64) * 64
        assert r0 + 10 * SLOT <= nc.sbuf_usable_end

        def place(name, slot, cols, dt=F32):
            return nc.alloc_sbuf_tensor_at(name, [P, cols], dt, offset=r0 + int(slot * SLOT))

        x_tok = place("x_tok", 0, TOK * D)
        xn = place("xn", 2, KT * S)
        sq_junk = place("sq_junk", 4, D)
        lx = place("lx", 0, BT * S)
        xc = place("xc", 1, BT * S)
        lr = place("lr", 2, BT * S)
        li = place("li", 3, BT * S)
        lg = place("lg", 4, BT * S)
        w_ga = place("w_ga", 9, BT * P)
        w_gx = place("w_gx", 9.5, BT * P)
        lru_hi = place("lru_hi", 1, BT * S, F32R)
        lru_lo = place("lru_lo", 2, BT * S, F32R)
        sb_ = place("sb_", 6, BT * S)
        sc_ = place("sc_", 5, BT * S)
        sv = place("sv", 0, BT * S)
        sc_hi = place("sc_hi", 3, BT * S, F32R)
        sc_lo = place("sc_lo", 4, BT * S, F32R)
        merged = place("merged", 7, KT * S)
        gate = place("gate", 9, GROUP * S)
        term = place("term", 9.5, GROUP * S)
        pu = place("pu", 5, BT * S)
        pa = place("pa", 6, BT * S)
        pb = place("pb", 0, BT * S)
        pool_hi = place("pool_hi", 1, BT * S, F32R)
        pool_lo = place("pool_lo", 2, BT * S, F32R)
        mg_hi = place("mg_hi", 3, KT * S, F32R)
        mg_lo = place("mg_lo", 5, KT * S, F32R)
        res = place("res", 1, TOK * D)
        nf_row = place("nf_row", 0, D)
        hst = place("hst", 7, KT * S)
        diag = place("diag", 9.5, TOK * P)
        rstd_bc = place("rstd_bc", 9.75, 2 * S)
        PF = PASSES[0] * GROUP
        f_hi = place("f_hi", 3, PF * S, F32R)
        f_lo = place("f_lo", 6, PF * S, F32R)
        silu = place("silu", 9, GROUP * S)
        f32_ = place("f32_", 9.5, GROUP * S)
        y_out = place("y_out", 3, TOK * CHUNK)
        y_first = g1_row
        pu_first = g2_row

        bank = [ctx.enter_context(nc.psum_tensor(f"bank{i}", [P, 2 * 512], F32)) for i in range(4)]

        raw_full = [sem(f"raw_full{i}") for i in range(RING)]
        hi_done = sem("hi_done")
        lo_done = sem("lo_done")
        chunk_used = sem("chunk_used")
        pair_full = [sem(f"pair_full{i}") for i in range(MOD_RING)]
        mod_full = [sem(f"mod_full{i}") for i in range(MOD_RING)]
        mod_used = sem("mod_used")
        side_done = {b: sem(f"side_done{b}") for b in (2, 3)}
        free = [sem(f"free{i}") for i in range(4)]
        par_in = sem("par_in")
        x_in = sem("x_in")
        gw_in = sem("gw_in")
        g2_in = sem("g2_in")
        rows_in = sem("rows_in")
        nf_in = sem("nf_in")
        res_in = sem("res_in")
        out_done = sem("out_done")
        ones_set = sem("ones_set")
        dve_order = sem("dve_order")
        silu_c_done = sem("silu_c_done")
        squared = sem("squared")
        sum_done = sem("sum_done")
        root_done = sem("root_done")
        normed = sem("normed")
        turned = sem("turned")
        first_tile = sem("first_tile")
        diag_done = sem("diag_done")
        spread = sem("spread")
        neg_abs_done = sem("neg_abs_done")
        exp_done = sem("exp_done")
        softplus_done = sem("softplus_done")
        conv_done = sem("conv_done")
        tanh_done = sem("tanh_done")
        ixc_done = sem("ixc_done")
        sqrt_done = sem("sqrt_done")
        lru_f32 = sem("lru_f32")
        lru_high = sem("lru_high")
        lru_low = sem("lru_low")
        sc_f32 = sem("sc_f32")
        sc_high = sem("sc_high")
        sc_low = sem("sc_low")
        pool_f32 = sem("pool_f32")
        pool_high = sem("pool_high")
        pool_low = sem("pool_low")
        aff_done = sem("aff_done")
        h_f32 = sem("h_f32")
        h_high = sem("h_high")
        h_low = sem("h_low")
        fin_done = sem("fin_done")
        mg_high = sem("mg_high")
        mg_low = sem("mg_low")
        f_high = sem("f_high")
        f_low = sem("f_low")
        res_done = sem("res_done")
        y_done = sem("y_done")
        rstd_done = sem("rstd_done")
        y_first_done = sem("y_first_done")

        def plus(const, step=0, i=0):
            return const + step * i if step else const

        block = ctx.enter_context(nc.Block())

        @block.sync
        def _(sync):
            def load(slot, chunk):
                return sync.dma_start(raw[slot][:, :], w_stream[chunk, :, :]).then_inc(raw_full[slot], 16)

            def load_mod(m):
                if m >= MOD_RING:
                    sync.wait_ge(mod_used, m - MOD_RING + 1)
                sync.dma_start(mod_raw[m % MOD_RING][:, :], m_stream[m, :, :]).then_inc(pair_full[m % MOD_RING], 16)

            sync.dma_start(par[:, :], params).then_inc(par_in, 16)
            chunk = 0
            for q in range(G_CHUNKS):
                for r in range(G_CHUNKS):
                    load_mod(q * G_CHUNKS + r)
                    if (q, r) in ((0, 5), (0, 7)) or (q and r in (2, 5, 7)):
                        for _ in range(1 if q else 2):
                            if chunk >= RING:
                                sync.wait_ge(lo_done, chunk - RING + 1)
                            load(chunk % RING, chunk)
                            chunk += 1
            for c in range(chunk, -(-chunk // RING) * RING):
                sync.wait_ge(lo_done, c - RING + 1)
                load(c % RING, c)
            with sync.Fori(-(-chunk // RING), N_CHUNKS // RING) as r:
                for c in range(RING):
                    sync.wait_ge(lo_done, 4 * r + (c - RING + 1))
                    sync.dma_start(raw[c][:, :],
                                   w_stream[bass.ds(4 * r + c, 1), :, :].rearrange("a p c -> p (a c)"))\
                        .then_inc(raw_full[c], 16)
            for t in range(TOK):
                sync.wait_ge(y_done, t + 1)
                sync.dma_start(out[t * P:(t + 1) * P, CHUNK:D], y_out[:, t * CHUNK:(t + 1) * CHUNK])\
                    .then_inc(out_done, 16)

        @block.gpsimd
        def _(pool):
            with pool.Fori(OPENING_MOD // MOD_RING, N_MOD // MOD_RING) as r:
                for c in range(MOD_RING):
                    pool.wait_ge(mod_used, 4 * r + (c - MOD_RING + 1))
                    pool.dma_start(mod_raw[c][:, :],
                                   m_stream[bass.ds(4 * r + c, 1), :, :].rearrange("a p c -> p (a c)"))\
                        .then_inc(mod_full[c], 16)

        @block.tensor
        def _(pe):
            def chunk_product(b, hi, lo, slot, k0, first_chunk, last_chunk):
                for kk in range(2):
                    act_hi, act_lo = (a[:, (k0 + kk) * S:(k0 + kk + 1) * S] for a in (hi, lo))
                    for m in range(GROUP):
                        acc = bank[b][:, m * S:(m + 1) * S]
                        cols = slice(kk * 512 + m * P, kk * 512 + (m + 1) * P)
                        first = first_chunk and kk == 0 and m % 2 == 0
                        nc.tensor.matmul(acc, w_hi[slot][:, cols], act_hi, start=first, stop=False,
                                         skip_group_check=True)
                        nc.tensor.matmul(acc, w_hi[slot][:, cols], act_lo, start=False, stop=False,
                                         skip_group_check=True)
                        mm = nc.tensor.matmul(acc, w_lo[slot][:, cols], act_hi, start=False,
                                              stop=last_chunk and kk == 1, skip_group_check=True)
                mm.then_inc(chunk_used, 1)

            def product(b, hi, lo, chunk, step, i, chunks, k0=0, ready=None):
                for c in range(chunks):
                    pe.wait_ge(lo_done, plus(chunk + c + 1, step, i))
                    if ready is not None:
                        pe.wait_ge(h_low, ready + c + 1)
                    chunk_product(b, hi, lo, (chunk + c) % RING, k0 + 2 * c, c == 0, c == chunks - 1)

            def wide(half, hi, lo, chunk, kts, uses, ready, midway=None):
                def tile(k, t):
                    b, slot = 2 * half + t, (chunk + k) % RING
                    if k == 0:
                        bank_free(b, uses[t])
                    cols = slice(k * S + t * P, k * S + (t + 1) * P)
                    for n, (act, w) in enumerate(((hi, w_hi), (hi, w_lo), (lo, w_hi))):
                        for q in range(2):
                            mm = nc.tensor.matmul(bank[b][:, q * 512:(q + 1) * 512], act[:, cols],
                                                  w[slot][:, q * 512:(q + 1) * 512],
                                                  start=(k == 0 and n == 0), stop=(k == kts - 1 and n == 2))
                    return mm

                def stand(k):
                    pe.wait_ge(lo_done, chunk + k + 1)
                    if k % GROUP == 0:
                        pe.wait_ge(ready[0], ready[1] + k // GROUP + 1)

                last = kts - RING if half else kts
                for k in range(last):
                    if k == kts // 2 and midway:
                        midway()
                    stand(k)
                    tile(k, 0)
                    tile(k, 1).then_inc(chunk_used, 1)
                if half:
                    for k in range(last, kts):
                        stand(k)
                        mm = tile(k, 0)
                    mm.then_inc(first_tile, 1)
                    for k in range(last, kts):
                        tile(k, 1).then_inc(chunk_used, 1)

            def wides(task, hi, lo, chunk, kts, ready, midway=None):
                wide(0, hi, lo, chunk, kts, pe_acc, ready)
                wide(1, hi, lo, chunk + kts, kts, [side_use(task, b)[1] for b in (2, 3)], ready, midway)

            def bank_free(b, uses):
                if uses:
                    pe.wait_ge(free[b], uses)

            def mod_half(task, m, row):
                b, uses, _ = side_use(task)
                bank_free(b, uses)
                pe.wait_ge(mod_used, MOD_HALF * (m + 1))
                if row:
                    pe.wait_ge(ones_set, 1)
                for j in range(CHUNK // P if not row else 2):
                    if row:
                        mm = nc.tensor.matmul(bank[b][:, j * 512:(j + 1) * 512], ones[:, :],
                                              mod_acc[m % 2][:, j * 512:(j + 1) * 512], start=True, stop=True)
                    else:
                        mm = nc.tensor.transpose(bank[b][:, j * P:(j + 1) * P],
                                                 mod_acc[m % 2][:, j * P:(j + 1) * P], ident[:, :])
                mm.then_inc(side_done[b], 1)

            def turn(b, src, quarter, tiles=range(TOK)):
                for t in tiles:
                    for j in range(GROUP):
                        at = t * D + (quarter * GROUP + j) * P
                        mm = nc.tensor.transpose(bank[b][:, j * S + t * P:j * S + (t + 1) * P],
                                                 src[:, at:at + P], ident[:, :])
                return mm

            pe.wait_ge(par_in, 32)
            pe.wait_ge(normed, TOK)
            def turn_input(q):
                b, uses, _ = side_use(f"x{q}")
                bank_free(b, uses)
                turn(b, x_tok, q).then_inc(side_done[b], 1)

            turn_input(0)
            turn_input(1)
            pe.wait_ge(ones_set, 1)
            groups = (0, 1, 3)
            for q in range(G_CHUNKS):
                b, uses, _ = side_use(f"s{q}")
                bank_free(b, uses)
                pe.wait_ge(mod_used, (q + 1) * G_CHUNKS)
                for j in range(GROUP):
                    for kk in range(2):
                        mm = nc.tensor.matmul(bank[b][:, j:j + 1], mod_acc[q % 2][:, kk * 512 + j * P:kk * 512 + (j + 1) * P],
                                              ones[:, 0:1], start=kk == 0, stop=kk == 1)
                mm.then_inc(side_done[b], 1)
                if q == 0:
                    turn_input(2)
                    turn_input(3)
                pe.wait_ge(h_low, q + 1)
                for n, b in enumerate(groups):
                    chunk = q * OPENING + n
                    pe.wait_ge(lo_done, chunk + 1)
                    if q == 0 and b == 3:
                        bank_free(b, side_use("pool")[1])
                    chunk_product(b, h_hi, h_lo, chunk % RING, 2 * q, q == 0, q == G_CHUNKS - 1)

            pe_acc = [1, 1]
            for b in range(2):
                bank_free(b, 1)
                product(b, h_hi, h_lo, PROJ + b * G_CHUNKS, 0, 0, G_CHUNKS)
            pe_acc = [2, 2]

            pe.wait_ge(gw_in, 32)
            pe.wait_ge(conv_done, BT)
            for name, w in (("r", w_ga), ("i", w_gx)):
                for half in range(2):
                    b, uses, _ = side_use(f"{name}{half}")
                    bank_free(b, uses)
                    for j in range(GROUP):
                        t = half * GROUP + j
                        mm = nc.tensor.matmul(bank[b][:, j * S:(j + 1) * S], w[:, t * P:(t + 1) * P],
                                              xc[:, t * S:(t + 1) * S], start=True, stop=True)
                    mm.then_inc(side_done[b], 1)

            with pe.Fori(0, A_GROUPS // 2 - 2) as i:
                for b in range(2):
                    pe.wait_ge(free[b], plus(pe_acc[b], 1, i))
                    product(b, h_hi, h_lo, PROJ + (2 + b) * G_CHUNKS, 2 * G_CHUNKS, i, G_CHUNKS)
            pe_acc = [n + A_GROUPS // 2 - 2 for n in pe_acc]
            mod_half("m4", 4, row=True)
            mod_half("m5", 5, row=True)

            def branch(chunk0, acts, ready):
                with pe.Fori(0, 4) as i:
                    pe.wait_ge(free[0], plus(pe_acc[0], 1, i))
                    product(0, h_hi, h_lo, chunk0, PAIR, i, G_CHUNKS)
                    pe.wait_ge(free[1], plus(pe_acc[1], 1, i))
                    pe.wait_ge(ready, 1)
                    product(1, *acts, chunk0 + G_CHUNKS, PAIR, i, OUT_CHUNKS)
                return [n + 4 for n in pe_acc]

            pe_acc = branch(LRU_OUT, (lru_hi, lru_lo), lru_low)
            mod_half("m6", 6, row=False)
            mod_half("m7", 7, row=False)

            bank_free(0, pe_acc[0])
            product(0, h_hi, h_lo, POOL_IN, 0, 0, G_CHUNKS)
            pe_acc[0] += 1
            pe_acc = branch(SC_OUT, (sc_hi, sc_lo), sc_low)
            mod_half("m8", 8, row=False)
            mod_half("m9", 9, row=False)

            for j in range(4):
                bank_free(0, pe_acc[0])
                product(0, h_hi, h_lo, POOL_OUT + j * POOL_PAIR, 0, 0, G_CHUNKS)
                bank_free(1, pe_acc[1])
                pe.wait_ge(pool_low, 1)
                product(1, pool_hi, pool_lo, POOL_OUT + j * POOL_PAIR + G_CHUNKS, 0, 0, 1, k0=2 * j)
                pe_acc = [n + 1 for n in pe_acc]

            def turn_first_half():
                pe.wait_ge(res_done, TOK)
                for q in range(2):
                    turn(q, res, q).then_inc(turned, 1)

            wides("wide_o", mg_hi, mg_lo, W_O, KT, (mg_low, 0), turn_first_half)
            pe_acc = [n + 2 for n in pe_acc]

            def spread_rstd(t):
                pe.wait_ge(diag_done, t + 1)
                for n in range(2):
                    mm = nc.tensor.matmul(bank[0][:, n * S + t * P:n * S + (t + 1) * P], ones[:, :],
                                          diag[:, t * P:(t + 1) * P], start=True, stop=True)
                mm.then_inc(spread, 1)

            pe.wait_ge(res_done, TOK + 1)
            turn(2, res, 2, (0,))
            bank_free(0, pe_acc[0])
            spread_rstd(0)
            bank_free(3, side_use("turn3")[1])
            turn(3, res, 3, (0,))
            pe.wait_ge(res_done, 2 * TOK)
            for q in (2, 3):
                turn(q, res, q, (1,)).then_inc(turned, 1)
            spread_rstd(1)
            pe_acc[0] += 1

            for p, groups in enumerate(PASSES):
                up, down = FFN[p]
                with pe.Fori(0, groups) as i:
                    for b in range(2):
                        pe.wait_ge(free[b], plus(pe_acc[b], 1, i))
                        product(b, h_hi, h_lo, up + b * G_CHUNKS, 2 * G_CHUNKS, i, G_CHUNKS,
                                ready=G_CHUNKS)
                pe_acc = [n + groups for n in pe_acc]
                if p == 0:
                    mod_half("m10", 10, row=True)
                    mod_half("m11", 11, row=True)
                wides(f"wide_f{p}", f_hi, f_lo, down, groups * GROUP, (f_low, sum(PASSES[:p])))
                pe_acc = [n + 1 for n in pe_acc]

        @block.scalar
        def _(act):
            act.dma_start(ident[:, :], ident_in).then_inc(par_in, 16)
            for t in range(TOK):
                act.dma_start(x_tok[:, t * D:(t + 1) * D], x[t * P:(t + 1) * P, :]).then_inc(x_in, 16)

            def high(chunk, step=0, i=0, n=1):
                for c in range(chunk, chunk + n):
                    if c >= N_CHUNKS:
                        return
                    act.wait_ge(raw_full[c % RING], plus(16 * (c // RING + 1), 16 * step // RING, i))
                    if c >= RING:
                        act.wait_ge(chunk_used, plus(c - RING + 1, step, i))
                    nc.scalar.activation(w_hi[c % RING][:, :], raw[c % RING][:, :], ACT.Copy).then_inc(hi_done, 1)

            act.wait_ge(par_in, 32)
            nc.scalar.activation(silu_c[:, :], par[:, P_C:P_C + KT], ACT.Silu).then_inc(silu_c_done, 1)
            act.wait_ge(neg_abs_done, 1)
            nc.scalar.activation(sp[:, BT:2 * BT], sp[:, 0:BT], ACT.Exp).then_inc(exp_done, 1)
            act.wait_ge(x_in, 32)
            act.wait_ge(ones_set, 1)

            def squares(junk, src, to, before):
                if before:
                    act.wait_ge(squared, before)
                nc.scalar.activation(junk, src, ACT.Square, accum_out=stat[:, to:to + 1]).then_inc(squared, 1)

            def root(src, to):
                nc.scalar.activation(stat[:, to], stat[:, src], ACT.Sqrt, bias=eps[:, 0:1], scale=1.0 / D)\
                    .then_inc(root_done, 1)

            for t in range(TOK):
                squares(sq_junk[:, :], x_tok[:, t * D:(t + 1) * D], t, t)
            act.wait_ge(squared, TOK)
            root(slice(0, 2), slice(2, 4))

            def take_input(q):
                b, _, done = side_use(f"x{q}")
                act.wait_ge(side_done[b], done)
                nc.scalar.activation(xn[:, q * CHUNK:(q + 1) * CHUNK], bank[b][:, :], ACT.Copy).then_inc(free[b], 1)

            def h_high_part(src, q, before):
                act.wait_ge(h_f32, before + 1)
                nc.scalar.activation(h_hi[:, q * 512:(q + 1) * 512], src[:, q * 512:(q + 1) * 512],
                                     ACT.Copy).then_inc(h_high, 1)

            take_input(0)
            take_input(1)
            high(0, n=OPENING)
            for q in range(G_CHUNKS):
                high((q + 1) * OPENING)
                if q % 2 == 0:
                    b, uses, _ = side_use(f"x{q // 2}")
                    act.wait_ge(free[b], uses + 1)
                act.wait_ge(aff_done, q + 1)
                for n in range(2):
                    part = xn[:, (2 * q + n) * S:(2 * q + n + 1) * S]
                    ins = nc.scalar.activation(part, part, ACT.Identity, scale=aff[:, 2 * q + n:2 * q + n + 1],
                                               bias=modc[:, 4 * q + 2 + n:4 * q + 3 + n])
                ins.then_inc(h_f32, 1)
                h_high_part(xn, q, q)
                if q == 0:
                    take_input(2)
                    take_input(3)
                high((q + 1) * OPENING + 1, n=OPENING - 1)
            act.dma_start(w_ga[:, :], gate_w[0]).then_inc(gw_in, 16)
            act.dma_start(w_gx[:, :], gate_w[1]).then_inc(gw_in, 16)
            act.dma_start(g1_row[:, :], rows[0:1, :].to_broadcast([P, D])).then_inc(rows_in, 16)
            act.dma_start(cnt[:, :], pool_cnt).then_inc(rows_in, 16)

            def take(dst, half, b, end, func=ACT.Copy):
                act.wait_ge(chunk_used, end)
                nc.scalar.activation(dst[:, half * CHUNK:(half + 1) * CHUNK], bank[b][:, :], func)\
                    .then_inc(free[b], 1)

            for b in range(2):
                take(lx, b, b, PROJ - OPENING + b + 1)
            take(pu_first, 0, 3, PROJ)
            high(PROJ + OPENING)

            def r_or_i(name, dst, bias):
                for half in range(2):
                    b, _, done = side_use(f"{name}{half}")
                    act.wait_ge(side_done[b], done)
                    for j in range(GROUP):
                        t = half * GROUP + j
                        ins = nc.scalar.activation(dst[:, t * S:(t + 1) * S], bank[b][:, j * S:(j + 1) * S],
                                                   ACT.Sigmoid, bias=par[:, bias + t:bias + t + 1])
                    ins.then_inc(free[b], 1)

            targets = [lx, lg, sb_, sc_]
            for g in range(2, A_GROUPS):
                high(PROJ + (g - 2) * G_CHUNKS + RING, n=G_CHUNKS)
                if g < 8:
                    take(targets[g // 2], g % 2, g % 2, PROJ + (g - 1) * G_CHUNKS,
                         ACT.Gelu_apprx_tanh if g // 2 == 1 else ACT.Copy)
                if g == 3:
                    r_or_i("r", lr, P_BA)
                    r_or_i("i", li, P_BX)
                    act.wait_ge(softplus_done, 1)
                    b, uses, _ = side_use("r1")
                    act.wait_ge(free[b], uses + 1)
                    for t in range(BT):
                        ins = nc.scalar.activation(lr[:, t * S:(t + 1) * S], lr[:, t * S:(t + 1) * S], ACT.Tanh,
                                                   scale=sp[:, 7 * BT + t:7 * BT + t + 1])
                    ins.then_inc(tanh_done, 1)
                    act.wait_ge(tanh_done, 1)
                if g == 4:
                    act.wait_ge(ixc_done, 1)
                    nc.scalar.activation(xc[:, :], lr[:, :], ACT.Sqrt).then_inc(sqrt_done, 1)
                if g == 7:
                    act.wait_ge(lru_f32, 1)
                    nc.scalar.activation(lru_hi[:, :], lg[:, :], ACT.Copy).then_inc(lru_high, 1)

            uses = [A_GROUPS // 2] * 2

            def sigmoid_gates(chunk_end, step, i, merged_before):
                act.wait_ge(chunk_used, plus(chunk_end, step, i))
                act.wait_ge(free[1], plus(merged_before, 1 if step else 0, i))
                nc.scalar.activation(gate[:, :], bank[0][:, :], ACT.Sigmoid).then_inc(free[0], 1)

            def gates(chunk0, merged_before):
                with act.Fori(0, 4) as i:
                    high(chunk0 + RING, PAIR, i, G_CHUNKS)
                    sigmoid_gates(chunk0 + G_CHUNKS, PAIR, i, merged_before)
                    high(chunk0 + RING + G_CHUNKS, PAIR, i, OUT_CHUNKS)

            gates(LRU_OUT, uses[1])
            uses = [n + 4 for n in uses]
            act.wait_ge(sc_f32, 1)
            nc.scalar.activation(sc_hi[:, :], sv[:, :], ACT.Copy).then_inc(sc_high, 1)
            high(POOL_IN + RING, n=G_CHUNKS)
            take(pu, 1, 0, POOL_IN + G_CHUNKS)
            uses[0] += 1
            gates(SC_OUT, uses[1])
            uses = [n + 4 for n in uses]
            act.wait_ge(pool_f32, 1)
            nc.scalar.activation(pool_hi[:, :], pa[:, :], ACT.Copy).then_inc(pool_high, 1)
            for j in range(4):
                chunk = POOL_OUT + j * POOL_PAIR
                high(chunk + RING, n=G_CHUNKS)
                sigmoid_gates(chunk + G_CHUNKS, 0, 0, uses[1] + j)
                high(chunk + RING + G_CHUNKS)
                act.wait_ge(fin_done, j + 1)
                nc.scalar.activation(mg_hi[:, j * CHUNK:(j + 1) * CHUNK], merged[:, j * CHUNK:(j + 1) * CHUNK],
                                     ACT.Copy).then_inc(mg_high, 1)
            uses = [n + 4 for n in uses]
            for t in range(TOK):
                act.dma_start(res[:, t * D:(t + 1) * D], x[t * P:(t + 1) * P, :]).then_inc(res_in, 16)
            act.dma_start(nf_row[:, :], rows[2:3, :].to_broadcast([P, D])).then_inc(nf_in, 16)
            act.dma_start(g2_row[:, :], rows[1:2, :].to_broadcast([P, D])).then_inc(g2_in, 16)

            def half_squares(half, t, to, res_before, squared_before):
                act.wait_ge(res_done, res_before + 1)
                o = t * D + half * CHUNK
                squares(silu[:, :], res[:, o:o + CHUNK], to + 2 * half + t, squared_before)

            high(W_O + RING, n=HALF_O + RING)
            for t in range(TOK):
                half_squares(0, t, 4, t, TOK + t)
            mid, end = W_O + HALF_O, W_O + 2 * HALF_O
            high(mid + 2 * RING, n=HALF_O // 2 - RING + 1)
            for q in range(2):
                act.wait_ge(turned, q + 1)
                nc.scalar.activation(hst[:, q * CHUNK:(q + 1) * CHUNK], bank[q][:, :], ACT.Copy).then_inc(free[q], 1)
            high(mid + HALF_O // 2 + RING + 1, n=HALF_O // 2 - RING - 1)
            for t in range(TOK):
                half_squares(1, t, 4, TOK + t, 2 * TOK + t)
                act.wait_ge(sum_done, t + 1)
                root(slice(8 + t, 9 + t), slice(10 + t, 11 + t))
                if t == 0:
                    high(end, n=RING)
            for q in range(G_CHUNKS):
                h_high_part(hst, q, G_CHUNKS + q)
            uses = [uses[0] + 3, uses[1] + 2]

            for p, groups in enumerate(PASSES):
                up, down = FFN[p]
                before = sum(PASSES[:p])
                with act.Fori(0, groups) as i:
                    high(up + RING, 2 * G_CHUNKS, i, G_CHUNKS)
                    act.wait_ge(chunk_used, plus(up + G_CHUNKS, 2 * G_CHUNKS, i))
                    act.wait_ge(free[1], plus(uses[1], 1, i))
                    nc.scalar.activation(silu[:, :], bank[0][:, :], ACT.Silu).then_inc(free[0], 1)
                    high(up + RING + G_CHUNKS, 2 * G_CHUNKS, i, G_CHUNKS)
                    act.wait_ge(free[1], plus(uses[1] + 1, 1, i))
                    nc.scalar.activation(f_hi[:, bass.ds(i * CHUNK, CHUNK)], f32_[:, :], ACT.Copy)\
                        .then_inc(f_high, 1)
                uses = [n + groups + 1 for n in uses]
                half = groups * GROUP
                high(down + RING, n=half + RING)
                if p:
                    for t in range(TOK):
                        half_squares(0, t, 12, 2 * TOK + t, 3 * TOK + t)
                high(down + half + 2 * RING, n=half - RING)

            for t in range(TOK):
                half_squares(1, t, 12, 3 * TOK + t, 4 * TOK + t)
                act.wait_ge(sum_done, TOK + t + 1)
                root(slice(16 + t, 17 + t), slice(18 + t, 19 + t))
                act.wait_ge(rstd_done, t + 1)
                part = y_first[:, t * CHUNK:(t + 1) * CHUNK]
                nc.scalar.activation(part, part, ACT.Copy, scale=stat[:, 18 + t:19 + t]).then_inc(y_first_done, 1)
                act.wait_ge(y_first_done, t + 1)
                act.dma_start(out[t * P:(t + 1) * P, 0:CHUNK], part).then_inc(out_done, 16)
            act.wait_ge(out_done, 32 * TOK)

        @block.vector
        def _(dve):
            def step(ins, done=dve_order):
                ins.then_inc(done, 1)
                stood[done.name] = stood.get(done.name, 0) + 1
                dve.wait_ge(done, stood[done.name])

            stood = {}
            V = nc.vector

            def low(chunk, stride=0, i=0, n=1):
                for c in range(chunk, chunk + n):
                    if c >= N_CHUNKS:
                        return
                    dve.wait_ge(hi_done, plus(c + 1, stride, i))
                    V.tensor_tensor(w_lo[c % RING][:, :], raw[c % RING][:, :], w_hi[c % RING][:, :].bitcast(F32),
                                    ALU.subtract).then_inc(lo_done, 1)

            def half_reduced(m):
                b, _, done = side_use(f"m{m}" if m >= 4 else f"s{m + G_CHUNKS - 4}")
                dve.wait_ge(side_done[b], done)

            def mod(m, n=1):
                for c in range(m, m + n):
                    k, acc = c % MOD_HALF, mod_acc[(c // MOD_HALF) % 2]
                    dve.wait_ge(mod_full[c % MOD_RING], 16 * ((c - OPENING_MOD) // MOD_RING + 1))
                    if k == 0:
                        half_reduced(c // MOD_HALF - 2)
                        V.tensor_scalar(acc[:, :], mod_raw[c % MOD_RING][:, :], silu_c[:, 0:1], None,
                                        ALU.mult).then_inc(mod_used, 1)
                    else:
                        dve.wait_ge(mod_used, c)
                        V.scalar_tensor_tensor(out=acc[:, :], in0=mod_raw[c % MOD_RING][:, :],
                                               scalar=silu_c[:, k:k + 1], in1=acc[:, :],
                                               op0=ALU.mult, op1=ALU.add).then_inc(mod_used, 1)

            def sums(task, dst, at):
                b, uses, done = side_use(task)
                dve.wait_ge(side_done[b], done)
                V.tensor_reduce(dst[:, at:at + CHUNK // P], bank[b][:, :].rearrange("p (j k) -> p j k", k=P),
                                AX.X, ALU.add).then_inc(free[b], 1)
                dve.wait_ge(free[b], uses + 1)

            def row_sums(task, dst, half):
                b, uses, done = side_use(task)
                dve.wait_ge(side_done[b], done)
                cols = slice(half * CHUNK, (half + 1) * CHUNK)
                V.tensor_tensor(dst[:, cols], bank[b][:, :], dst[:, cols], ALU.add).then_inc(free[b], 1)
                dve.wait_ge(free[b], uses + 1)

            def affine(sc_at, sh_at, b_sc, b_sh, norm, to):
                step(V.tensor_tensor(modc[:, sc_at:sc_at + KT], modc[:, sc_at:sc_at + KT],
                                     par[:, P_BMOD + b_sc * KT:P_BMOD + (b_sc + 1) * KT], ALU.add))
                step(V.scalar_tensor_tensor(out=aff[:, to:to + KT], in0=modc[:, sc_at:sc_at + KT], scalar=1.0,
                                            in1=par[:, norm:norm + KT], op0=ALU.add, op1=ALU.mult))
                step(V.tensor_tensor(aff[:, to + KT:to + 2 * KT], modc[:, sh_at:sh_at + KT],
                                     par[:, P_BMOD + b_sh * KT:P_BMOD + (b_sh + 1) * KT], ALU.add))

            V.memset(eps[:, :], EPS).then_inc(dve_order, 1)
            V.memset(ones[:, :], 1.0).then_inc(ones_set, 1)
            stood[dve_order.name] = 1
            dve.wait_ge(dve_order, 1)
            dve.wait_ge(ones_set, 1)
            dve.wait_ge(par_in, 32)
            lam = par[:, P_LAM:P_LAM + BT]

            def spc(i):
                return sp[:, i * BT:(i + 1) * BT]

            step(V.tensor_scalar(spc(2), lam, -1.0, 0.0, ALU.mult, ALU.max))
            step(V.scalar_tensor_tensor(out=spc(0), in0=spc(2), scalar=-2.0, in1=lam, op0=ALU.mult,
                                        op1=ALU.subtract), neg_abs_done)

            def mod_pair(q, r):
                m = q * G_CHUNKS + r
                acc, src = mod_acc[q % 2], mod_raw[m % MOD_RING]
                dve.wait_ge(pair_full[m % MOD_RING], 16 * (m // MOD_RING + 1))
                if r == 0 and q >= 2:
                    b, _, done = side_use(f"s{q - 2}")
                    dve.wait_ge(side_done[b], done)
                if r == 0 and q < 2:
                    dve.wait_ge(silu_c_done, 1)
                if r:
                    dve.wait_ge(mod_used, m)
                for kk in range(2):
                    k, cols = 2 * r + kk, slice(kk * 512, (kk + 1) * 512)
                    if r == 0:
                        ins = V.tensor_scalar(acc[:, cols], src[:, cols], silu_c[:, k:k + 1], None, ALU.mult)
                    else:
                        ins = V.scalar_tensor_tensor(out=acc[:, cols], in0=src[:, cols], scalar=silu_c[:, k:k + 1],
                                                     in1=acc[:, cols], op0=ALU.mult, op1=ALU.add)
                ins.then_inc(mod_used, 1)

            for r in range(2):
                mod_pair(0, r)
            dve.wait_ge(exp_done, 1)
            step(V.tensor_scalar(spc(3), spc(1), 2.0, None, ALU.add))
            step(V.reciprocal(spc(3), spc(3)))
            step(V.tensor_tensor(spc(3), spc(3), spc(1), ALU.mult))
            step(V.tensor_tensor(spc(4), spc(3), spc(3), ALU.mult))
            step(V.memset(spc(5), 1.0 / 17))
            for n in range(15, 0, -2):
                step(V.tensor_tensor(spc(5), spc(5), spc(4), ALU.mult))
                step(V.tensor_scalar(spc(5), spc(5), 1.0 / n, None, ALU.add))
            step(V.tensor_tensor(spc(5), spc(5), spc(3), ALU.mult))
            step(V.scalar_tensor_tensor(out=spc(6), in0=spc(5), scalar=2.0, in1=spc(2), op0=ALU.mult, op1=ALU.add))
            step(V.tensor_scalar(spc(7), spc(6), 4.0, None, ALU.mult), softplus_done)
            for r in range(2, 4):
                mod_pair(0, r)
            dve.wait_ge(root_done, 1)
            step(V.reciprocal(stat[:, 2:4], stat[:, 2:4]))
            for t in range(TOK):
                step(V.tensor_scalar(x_tok[:, t * D:(t + 1) * D], x_tok[:, t * D:(t + 1) * D],
                                     stat[:, 2 + t:3 + t], None, ALU.mult), normed)
            for r in range(4, G_CHUNKS):
                mod_pair(0, r)
            low(0, n=OPENING)

            def h_pair(q):
                b, uses, done = side_use(f"s{q}")
                both, k = modc[:, 4 * q:4 * q + 4], 2 * q
                dve.wait_ge(side_done[b], done)
                V.tensor_tensor(both, bank[b][:, 0:4], par[:, P_B1 + 4 * q:P_B1 + 4 * q + 4], ALU.add)\
                    .then_inc(free[b], 1)
                dve.wait_ge(free[b], uses + 1)
                step(V.scalar_tensor_tensor(out=aff[:, k:k + 2], in0=both[:, 0:2], scalar=1.0,
                                            in1=par[:, P_NMIX + k:P_NMIX + k + 2], op0=ALU.add, op1=ALU.mult),
                     aff_done)

            def h_low_part(src, q, before):
                dve.wait_ge(h_high, before + 1)
                V.tensor_tensor(h_lo[:, q * 512:(q + 1) * 512], src[:, q * 512:(q + 1) * 512],
                                h_hi[:, q * 512:(q + 1) * 512].bitcast(F32), ALU.subtract).then_inc(h_low, 1)

            for q in range(G_CHUNKS):
                following = iter(range(G_CHUNKS)) if q + 1 < G_CHUNKS else iter(())

                def next_mod(n):
                    for _, r in zip(range(n), following):
                        mod_pair(q + 1, r)

                next_mod(1)
                h_pair(q)
                low((q + 1) * OPENING)
                next_mod(1)
                h_low_part(xn, q, q)
                next_mod(3)
                for c in range(1, OPENING):
                    low((q + 1) * OPENING + c)
                    next_mod(3 - c)
            low(PROJ + OPENING)

            def three_d(t):
                return t[:, :].rearrange("p (j s) -> p j s", s=S)

            def conv(dst, src, tiles, taps, width, bias=None, done=dve_order):
                for t in tiles:
                    o, u = t * S, (t + 1) * S
                    w = taps + (width - 1) * BT + t
                    if bias is None:
                        step(V.tensor_scalar(dst[:, o:u], src[:, o:u], par[:, w:w + 1], None, ALU.mult))
                    else:
                        step(V.tensor_scalar(dst[:, o:u], src[:, o:u], par[:, w:w + 1],
                                             par[:, bias + t:bias + t + 1], ALU.mult, ALU.add))
                    for back in range(1, width):
                        w = taps + (width - 1 - back) * BT + t
                        step(V.scalar_tensor_tensor(out=dst[:, o + back:u], in0=src[:, o:u - back],
                                                    scalar=par[:, w:w + 1], in1=dst[:, o + back:u],
                                                    op0=ALU.mult, op1=ALU.add),
                             done if back == width - 1 else dve_order)

            mods = [0, 0, 2, 5, 6, 4, 3, 5, 4, 3]
            m, t_conv = OPENING_MOD, 0
            for b in range(2):
                dve.wait_ge(free[b], 1)
            for g in range(2, A_GROUPS):
                for c in range(G_CHUNKS):
                    low(PROJ + (g - 2) * G_CHUNKS + RING + c)
                    if (c + 1) * mods[g] // G_CHUNKS > c * mods[g] // G_CHUNKS:
                        mod(m)
                        m += 1
                    if t_conv < BT and (g == 2 and c % 3 < 2 or g == 3 and c < 3):
                        conv(xc, lx, (t_conv,), P_CONVW, 4, P_CONVB, conv_done)
                        t_conv += 1
                    if g == 4 and c == 4:
                        dve.wait_ge(tanh_done, 1)
                        step(V.tensor_tensor(li[:, :], li[:, :], xc[:, :], ALU.mult), ixc_done)
                    if g == 4 and c == 6:
                        step(V.tensor_scalar(lx[:, :], lr[:, :], 1.0, None, ALU.add))
                    if g == 5 and c % 2 == 0:
                        part = lx[:, c // 2 * 512:(c // 2 + 1) * 512]
                        step(V.reciprocal(part, part))
                    if g == 6 and c == 0:
                        dve.wait_ge(sqrt_done, 1)
                        step(V.scalar_tensor_tensor(out=xc[:, :], in0=xc[:, :], scalar=2.0, in1=lx[:, :],
                                                    op0=ALU.mult, op1=ALU.mult))
                        step(V.memset(three_d(xc)[:, :, 0:1], 1.0))
                    if g == 6 and c == 2:
                        step(V.tensor_tensor(li[:, :], li[:, :], xc[:, :], ALU.mult))
                    if g == 6 and c == 4:
                        step(V.tensor_scalar(lr[:, :], lr[:, :], -1.0, 1.0, ALU.mult, ALU.add))
                    if g == 6 and c == 6:
                        step(V.tensor_tensor(lr[:, :], lr[:, :], lx[:, :], ALU.mult))
                        step(V.memset(three_d(lr)[:, :, 0:1], 0.0))
                    if g == 7 and c == 0:
                        step(V.tensor_tensor_scan(lx[:, :], lr[:, :], li[:, :], 0.0, ALU.mult, ALU.add))
                    if g == 7 and c == 4:
                        step(V.tensor_tensor(lg[:, :], lg[:, :], lx[:, :], ALU.mult), lru_f32)
                    if g == 8 and c == 4:
                        dve.wait_ge(lru_high, 1)
                        step(V.tensor_tensor(lru_lo[:, :], lg[:, :], lru_hi[:, :].bitcast(F32), ALU.subtract),
                             lru_low)
                if g >= 8:
                    b = g % 2
                    cols = slice(b * CHUNK, (b + 1) * CHUNK)
                    dve.wait_ge(chunk_used, PROJ + (g - 1) * G_CHUNKS)
                    V.tensor_tensor(sc_[:, cols], bank[b][:, :], sc_[:, cols], ALU.mult).then_inc(free[b], 1)
            dve.wait_ge(rows_in, 32)
            row_sums("m4", g1_row, 0)
            row_sums("m5", g1_row, 1)

            def merge(j, uses, branch_no, chunk_end):
                dst = merged[:, j * CHUNK:(j + 1) * CHUNK]
                dve.wait_ge(free[0], uses[0] + j + 1)
                dve.wait_ge(chunk_used, chunk_end)
                if branch_no == 0:
                    V.tensor_tensor(dst, bank[1][:, :], gate[:, :], ALU.mult).then_inc(free[1], 1)
                    return
                if branch_no == 1:
                    V.tensor_tensor(term[:, :], bank[1][:, :], gate[:, :], ALU.mult).then_inc(free[1], 1)
                else:
                    for m in range(GROUP):
                        cols = slice(m * S, (m + 1) * S)
                        at = P_PSCALE + j * GROUP + m
                        ins = V.scalar_tensor_tensor(out=term[:, cols], in0=bank[1][:, cols],
                                                     scalar=par[:, at:at + 1], in1=gate[:, cols],
                                                     op0=ALU.mult, op1=ALU.mult)
                    ins.then_inc(free[1], 1)
                dve.wait_ge(free[1], uses[1] + j + 1)
                step(V.tensor_tensor(dst, dst, term[:, :], ALU.add), fin_done if branch_no == 2 else dve_order)

            uses = [A_GROUPS // 2] * 2
            for j in range(4):
                for c in range(PAIR):
                    low(LRU_OUT + j * PAIR + RING + c)
                    if c < 8:
                        mod(96 + 8 * j + c)
                    if c in (9, 10):
                        conv(sv, sc_, (2 * j + c - 9,), P_SCW, 3)
                merge(j, uses, 0, LRU_OUT + (j + 1) * PAIR)
            uses = [n + 4 for n in uses]
            sums("m6", modc, 2 * KT)
            sums("m7", modc, 2 * KT + CHUNK // P)
            step(V.tensor_tensor(sv[:, :], sv[:, :], sb_[:, :], ALU.mult), sc_f32)
            low(POOL_IN + RING)
            dve.wait_ge(sc_high, 1)
            step(V.tensor_tensor(sc_lo[:, :], sv[:, :], sc_hi[:, :].bitcast(F32), ALU.subtract), sc_low)
            low(POOL_IN + RING + 1, n=G_CHUNKS - 1)
            uses[0] += 1

            def pool_means():
                tiles = BT // 4
                for g, window in enumerate(POOL_WINDOWS):
                    cols = slice(g * tiles * S, (g + 1) * tiles * S)
                    u = pu_first if g < 2 else pu
                    src, w = u, 1
                    for dst in (pa, pb, pa, pb)[:g + 1]:
                        s3 = src[:, cols].rearrange("p (j s) -> p j s", s=S)
                        d3 = dst[:, cols].rearrange("p (j s) -> p j s", s=S)
                        step(V.tensor_tensor(d3[:, :, w:], s3[:, :, w:], s3[:, :, :S - w], ALU.add))
                        step(V.tensor_copy(d3[:, :, 0:w], s3[:, :, 0:w]))
                        src, w = dst, 2 * w
                    dst = pa
                    s3 = src[:, cols].rearrange("p (j s) -> p j s", s=S)
                    at = sum(POOL_WINDOWS[:g])
                    for j in range(tiles):
                        step(V.tensor_tensor(s3[:, j, 0:window], s3[:, j, 0:window], cnt[:, at:at + window],
                                             ALU.mult))
                    step(V.scalar_tensor_tensor(out=dst[:, cols], in0=src[:, cols], scalar=1.0 / window,
                                                in1=u[:, cols], op0=ALU.mult, op1=ALU.subtract),
                         pool_f32 if g == 3 else dve_order)
                    yield

            dve.wait_ge(free[0], uses[0])
            dve.wait_ge(free[3], side_use("pool")[1] + 1)
            pooling = pool_means()
            for j in range(4):
                for c in range(PAIR):
                    low(SC_OUT + j * PAIR + RING + c)
                    if c < 8:
                        mod(128 + 8 * j + c)
                    if c == 9:
                        next(pooling)
                merge(j, uses, 1, SC_OUT + (j + 1) * PAIR)
            uses = [n + 4 for n in uses]
            sums("m8", modc, 3 * KT)
            sums("m9", modc, 3 * KT + CHUNK // P)
            affine(3 * KT, 2 * KT, 4, 3, P_NFFN, KT)

            low(POOL_OUT + RING)
            dve.wait_ge(pool_high, 1)
            step(V.tensor_tensor(pool_lo[:, :], pa[:, :], pool_hi[:, :].bitcast(F32), ALU.subtract), pool_low)
            for j in range(4):
                low(POOL_OUT + j * POOL_PAIR + RING + (j == 0), n=POOL_PAIR - (j == 0))
                merge(j, uses, 2, POOL_OUT + (j + 1) * POOL_PAIR)
                dve.wait_ge(mg_high, j + 1)
                V.tensor_tensor(mg_lo[:, j * CHUNK:(j + 1) * CHUNK], merged[:, j * CHUNK:(j + 1) * CHUNK],
                                mg_hi[:, j * CHUNK:(j + 1) * CHUNK].bitcast(F32), ALU.subtract).then_inc(mg_low, 1)
            uses = [n + 4 for n in uses]

            def row_sum(src, to, t, before):
                dve.wait_ge(squared, before + 2 * 1 + t + 1)
                step(V.tensor_tensor(stat[:, to + t:to + t + 1], stat[:, src + t:src + t + 1],
                                     stat[:, src + 2 + t:src + 3 + t], ALU.add), sum_done)

            def update(half, t, g_row, before, done, final=False):
                b, cols = 2 * half + t, slice(half * CHUNK, (half + 1) * CHUNK)
                part = res[:, t * D + half * CHUNK:t * D + (half + 1) * CHUNK]
                V.tensor_tensor(mod_acc[t][:, :], bank[b][:, :], g_row[:, cols], ALU.mult).then_inc(free[b], 1)
                dve.wait_ge(free[b], before + 1)
                step(V.tensor_tensor(part, part, mod_acc[t][:, :], ALU.add), done)
                if final:
                    y = (y_out if half else y_first)[:, t * CHUNK:(t + 1) * CHUNK]
                    step(V.tensor_tensor(y, part, nf_row[:, cols], ALU.mult))

            def updates(chunk, half, uses, g_row, task, done, final=False, tile_done=None):
                mid, end = chunk + half, chunk + 2 * half
                low(chunk + RING, n=half)
                dve.wait_ge(chunk_used, mid)
                for t in range(TOK):
                    update(0, t, g_row, uses[t], done, final)
                low(mid + RING, n=half - RING)
                dve.wait_ge(first_tile, 1 + ("wide_o", "wide_f0", "wide_f1").index(task))
                update(1, 0, g_row, side_use(task, 2)[1], done, final)
                if tile_done:
                    tile_done(0)
                low(end, n=RING - 1)
                dve.wait_ge(chunk_used, end)
                update(1, 1, g_row, side_use(task, 3)[1], done, final)
                low(end + RING - 1)
                if tile_done:
                    tile_done(1)

            half_reduced(8)
            half_reduced(9)
            dve.wait_ge(res_in, 32)

            def rstd2(t):
                row_sum(4, 8, t, TOK)
                dve.wait_ge(root_done, 2 + t)
                r = stat[:, 10 + t:11 + t]
                step(V.reciprocal(r, r))
                step(V.tensor_scalar(diag[:, t * P:(t + 1) * P], ident[:, :], r, None, ALU.mult), diag_done)

            updates(W_O, HALF_O, uses, g1_row, "wide_o", res_done, tile_done=rstd2)

            dve.wait_ge(spread, TOK)
            V.tensor_copy(rstd_bc[:, :], bank[0][:, 0:2 * S]).then_inc(free[0], 1)
            dve.wait_ge(free[0], uses[0] + 3)
            dve.wait_ge(free[1], uses[1] + 2)
            for q in range(G_CHUNKS):
                pair = hst[:, q * 512:(q + 1) * 512]
                if q < 4:
                    step(V.tensor_tensor(pair, pair, rstd_bc[:, :], ALU.mult))
                else:
                    b = q // 2
                    dve.wait_ge(turned, b + 1)
                    ins = V.tensor_tensor(pair, bank[b][:, q % 2 * 512:(q % 2 + 1) * 512], rstd_bc[:, :], ALU.mult)
                    if q % 2:
                        ins.then_inc(free[b], 1)
                        dve.wait_ge(free[b], side_use(f"turn{b}")[1] + 1)
                    else:
                        step(ins)
                for k in (2 * q, 2 * q + 1):
                    part = hst[:, k * S:(k + 1) * S]
                    ins = V.tensor_scalar(part, part, aff[:, KT + k:KT + k + 1], aff[:, 2 * KT + k:2 * KT + k + 1],
                                          ALU.mult, ALU.add)
                ins.then_inc(h_f32, 1)
                if q:
                    h_low_part(hst, q - 1, G_CHUNKS + q - 1)
            h_low_part(hst, G_CHUNKS - 1, 2 * G_CHUNKS - 1)
            uses = [uses[0] + 3, uses[1] + 2]

            def final_norm(t):
                row_sum(12, 16, t, 3 * TOK)
                dve.wait_ge(root_done, 4 + t)
                r, y = stat[:, 18 + t:19 + t], y_out[:, t * CHUNK:(t + 1) * CHUNK]
                step(V.reciprocal(r, r), rstd_done)
                step(V.tensor_scalar(y, y, r, None, ALU.mult), y_done)

            for p, groups in enumerate(PASSES):
                up, down = FFN[p]
                before = sum(PASSES[:p])

                def hidden(i, mods):
                    for c in range(2 * G_CHUNKS):
                        low(up + RING + c, 2 * G_CHUNKS, i)
                        if mods and c % 2:
                            mod(160 + 8 * i + c // 2)
                    dve.wait_ge(free[0], plus(uses[0] + 1, 1, i))
                    dve.wait_ge(chunk_used, plus(up + 2 * G_CHUNKS, 2 * G_CHUNKS, i))
                    V.tensor_tensor(f32_[:, :], bank[1][:, :], silu[:, :], ALU.mult).then_inc(free[1], 1)
                    dve.wait_ge(f_high, plus(before + 1, 1, i))
                    hid = f_hi[:, bass.ds(i * CHUNK, CHUNK)]
                    V.tensor_tensor(f_lo[:, bass.ds(i * CHUNK, CHUNK)], f32_[:, :], hid.bitcast(F32), ALU.subtract)\
                        .then_inc(f_low, 1)

                first = 0
                if p == 0:
                    first = 4
                    for i in range(first):
                        hidden(i, True)
                with dve.Fori(first, groups) as i:
                    hidden(i, False)
                uses = [n + groups for n in uses]
                if p == 0:
                    dve.wait_ge(g2_in, 16)
                    row_sums("m10", g2_row, 0)
                    row_sums("m11", g2_row, 1)
                half = groups * GROUP
                if p:
                    dve.wait_ge(nf_in, 16)
                updates(down, half, uses, g2_row, f"wide_f{p}", res_done if p else dve_order, bool(p),
                        final_norm if p else None)
                uses = [n + 1 for n in uses]


_WEIGHTS = ["w_in", "lru_w_out", "sc_w_out", "pool_w", "w_o", "ffn_w1", "ffn_w3", "ffn_w2"]


def _group(np, w, col):
    k = w.shape[0] // (2 * P)
    return w[:, col:col + 512].reshape(k, 2, P, 512).transpose(0, 2, 1, 3).reshape(k, P, CHUNK)


def _half(np, w, half):
    return w[:, half * CHUNK:(half + 1) * CHUNK].reshape(-1, P, CHUNK)


def _weight_stream(np, w):
    w_in, proj = w["w_in"], 2 * W_LRU + 4 * W_LRU
    opening = np.stack([_group(np, w_in, g * 512) for g in (0, 1, A_GROUPS)], axis=1)
    parts = [opening.reshape(-1, P, CHUNK)] + [_group(np, w_in, g * 512) for g in range(2, A_GROUPS)]
    for j in range(4):
        parts += [_group(np, w_in, proj + j * 512), _group(np, w["lru_w_out"], j * 512)]
    parts += [_group(np, w_in, (A_GROUPS + 1) * 512)]
    for j in range(4):
        parts += [_group(np, w_in, proj + D + j * 512), _group(np, w["sc_w_out"], j * 512)]
    for j in range(4):
        parts += [_group(np, w_in, proj + 2 * D + j * 512), _group(np, w["pool_w"][j], 0)]
    parts += [_half(np, w["w_o"], h) for h in range(2)]
    first = 0
    for groups in PASSES:
        for g in range(first, first + groups):
            parts += [_group(np, w["ffn_w1"], g * 512), _group(np, w["ffn_w3"], g * 512)]
        parts += [_half(np, w["ffn_w2"][first * 512:(first + groups) * 512], h) for h in range(2)]
        first += groups
    return np.concatenate(parts)


def kernel(**inputs):
    import numpy as np
    import concourse.bacc as bacc
    from concourse.bass_utils import run_bass_kernel_spmd

    a = {k: np.asarray(v) for k, v in inputs.items()}
    w_stream = _weight_stream(np, {k: a[k][0] for k in _WEIGHTS})
    assert w_stream.shape == (N_CHUNKS, P, CHUNK)
    halves = a["w_mod"][0].reshape(KT, P, 2 * len(MOD_ORDER), CHUNK).transpose(2, 0, 1, 3)
    scale_shift = a["w_mod"][0][:, :2 * D].reshape(KT // 2, 2, P, 2, KT // 2, 2 * P)[:, :, :, ::-1]
    opening = scale_shift.transpose(4, 0, 2, 1, 3, 5).reshape(-1, P, CHUNK)
    m_stream = np.concatenate([opening] + [halves[2 * v + h] for v in MOD_ORDER[2:] for h in range(2)])

    def cols(v):
        return v.reshape(-1, P).T

    params = np.ascontiguousarray(np.concatenate([
        cols(a["b_mod"]), cols(a["norm_mix"]), cols(a["norm_ffn"]), cols(a["pool_scale"]), cols(a["lru_conv_w"]),
        cols(a["lru_conv_b"]), cols(a["lru_b_a"]), cols(a["lru_b_x"]), cols(a["lru_lambda"]),
        cols(a["sc_conv_w"]), cols(a["c"]),
        cols(a["b_mod"])[:, :2 * KT].reshape(P, 2, KT // 2, 2)[:, ::-1].transpose(0, 2, 1, 3).reshape(P, 2 * KT)],
        axis=1))
    assert params.shape == (P, N_PARAM)
    gate_w = np.zeros((2, P, BT, P), np.float32)
    for n, name in enumerate(("lru_w_a", "lru_w_x")):
        for head in range(2 * BT):
            o = (head % 2) * 64
            gate_w[n, o:o + 64, head // 2, o:o + 64] = a[name][0, head]
    b_mod = a["b_mod"].reshape(-1, D)
    rows = np.ascontiguousarray(np.stack([b_mod[2], b_mod[5], a["norm_final"]]))
    pool_cnt = np.tile(np.concatenate([w / np.arange(1, w + 1) for w in POOL_WINDOWS]).astype(np.float32), (P, 1))
    arrays = {
        "x": np.ascontiguousarray(a["x"][0]), "params": params, "gate_w": gate_w.reshape(2, P, BT * P),
        "rows": rows, "pool_cnt": pool_cnt, "w_stream": w_stream, "m_stream": m_stream,
        "ident": np.eye(P, dtype=np.float32),
    }
    nc = bacc.Bacc("TRN2", target_bir_lowering=False, num_devices=1)
    args = [nc.dram_tensor(f"in_{k}", v.shape, F32, kind="ExternalInput").ap() for k, v in arrays.items()]
    out = nc.dram_tensor("out_y", (S, D), F32, kind="ExternalOutput").ap()
    trunk_kernel(nc, *args, out)
    result = run_bass_kernel_spmd(nc, [{f"in_{k}": v for k, v in arrays.items()}], core_ids=[0])
    return result.results[0]["out_y"].reshape(1, S, D)
```

```python
from contextlib import ExitStack

import concourse.bass as bass
from concourse import mybir

F32 = mybir.dt.float32
F32R = mybir.dt.float32r
ALU = mybir.AluOpType
ACT = mybir.ActivationFunctionType
AX = mybir.AxisListType

P = 128
D = 2048
S = 256
FF = 5632
EPS = 1e-6
KT = D // P
TOK = S // P
W_LRU = 1024
BT = W_LRU // P
CHUNK = 1024
GROUP = 4
RING = 4
MOD_RING = 4
POOL_WINDOWS = (2, 4, 8, 16)

G_CHUNKS = KT // 2
OUT_CHUNKS = BT // 2
A_GROUPS = 10
OPENING = 3
PROJ = OPENING * G_CHUNKS
LRU_OUT = PROJ + (A_GROUPS - 2) * G_CHUNKS
PAIR = G_CHUNKS + OUT_CHUNKS
POOL_IN = LRU_OUT + 4 * PAIR
SC_OUT = POOL_IN + G_CHUNKS
POOL_OUT = SC_OUT + 4 * PAIR
POOL_PAIR = G_CHUNKS + 1
W_O = POOL_OUT + 4 * POOL_PAIR
HALF_O = KT
PASSES = (6, 5)
assert sum(PASSES) * 512 == FF
FFN = []
_n = W_O + 2 * HALF_O
for _g in PASSES:
    FFN.append((_n, _n + _g * 2 * G_CHUNKS))
    _n = FFN[-1][1] + 2 * GROUP * _g
N_CHUNKS = _n
MOD_HALF = KT
MOD_ORDER = (1, 0, 2, 3, 4, 5)
N_MOD = 2 * MOD_HALF * len(MOD_ORDER)
OPENING_MOD = 4 * MOD_HALF

P_BMOD = 0
P_NMIX = 96
P_NFFN = 112
P_PSCALE = 128
P_CONVW = 144
P_CONVB = 176
P_BA = 184
P_BX = 192
P_LAM = 200
P_SCW = 208
P_C = 232
P_B1 = 248
N_PARAM = 280

SIDE = [("x0", 3), ("s0", 2), ("x1", 3), ("x2", 2), ("x3", 3), ("pool", 3)] + [
    (f"s{q}", 2) for q in range(1, G_CHUNKS)] + [
    ("r0", 2), ("r1", 3), ("i0", 2), ("i1", 3), ("m4", 2), ("m5", 3), ("m6", 2), ("m7", 3), ("m8", 2), ("m9", 3),
    ("wide_o", 2), ("wide_o", 3), ("turn2", 2), ("turn3", 3), ("m10", 2), ("m11", 3), ("wide_f0", 2),
    ("wide_f0", 3), ("wide_f1", 2), ("wide_f1", 3)]


def side_use(task, bank=None):
    bank = bank or dict(SIDE)[task]
    before = [t for t, b in SIDE[:SIDE.index((task, bank))] if b == bank]
    return bank, len(before), 1 + sum(not t.startswith(("wide", "pool", "turn")) for t in before)


def trunk_kernel(nc, x, params, gate_w, rows, pool_cnt, w_stream, m_stream, ident_in, out):
    with ExitStack() as ctx:

        def sb(name, cols, dt=F32, at=None):
            return ctx.enter_context(nc.sbuf_tensor(name, [P, cols], dt)) if at is None else \
                nc.alloc_sbuf_tensor_at(name, [P, cols], dt, offset=at)

        def sem(name):
            return ctx.enter_context(nc.semaphore(name))

        raw = [sb(f"raw{i}", CHUNK) for i in range(RING)]
        w_hi = [sb(f"w_hi{i}", CHUNK, F32R) for i in range(RING)]
        w_lo = [sb(f"w_lo{i}", CHUNK, F32R) for i in range(RING)]
        mod_raw = [sb(f"mod_raw{i}", CHUNK) for i in range(MOD_RING)]
        h_hi = sb("h_hi", KT * S, F32R)
        h_lo = sb("h_lo", KT * S, F32R)
        mod_acc = [sb(f"mod_acc{i}", CHUNK) for i in range(2)]
        g1_row = sb("g1_row", D)
        g2_row = sb("g2_row", D)
        par = sb("par", N_PARAM)
        modc = sb("modc", 4 * KT)
        aff = sb("aff", 3 * KT)
        silu_c = sb("silu_c", KT)
        sp = sb("sp", 8 * BT)
        stat = sb("stat", 22)
        eps = sb("eps", 1)
        no_use = sb("no_use", 1)
        ident = sb("ident", P)
        ones = sb("ones", P)
        cnt = sb("cnt", sum(POOL_WINDOWS))

        SLOT = D * 4
        r0 = -(-nc.sbuf_base // 64) * 64
        assert r0 + 10 * SLOT <= nc.sbuf_usable_end

        def place(name, slot, cols, dt=F32):
            return nc.alloc_sbuf_tensor_at(name, [P, cols], dt, offset=r0 + int(slot * SLOT))

        x_tok = place("x_tok", 0, TOK * D)
        xn = place("xn", 2, KT * S)
        sq_junk = place("sq_junk", 4, D)
        lx = place("lx", 0, BT * S)
        xc = place("xc", 1, BT * S)
        lr = place("lr", 2, BT * S)
        li = place("li", 3, BT * S)
        lg = place("lg", 4, BT * S)
        w_ga = place("w_ga", 9, BT * P)
        w_gx = place("w_gx", 9.5, BT * P)
        lru_hi = place("lru_hi", 1, BT * S, F32R)
        lru_lo = place("lru_lo", 2, BT * S, F32R)
        sb_ = place("sb_", 6, BT * S)
        sc_ = place("sc_", 5, BT * S)
        sv = place("sv", 0, BT * S)
        sc_hi = place("sc_hi", 3, BT * S, F32R)
        sc_lo = place("sc_lo", 4, BT * S, F32R)
        merged = place("merged", 7, KT * S)
        gate = place("gate", 9, GROUP * S)
        term = place("term", 9.5, GROUP * S)
        pu = place("pu", 5, BT * S)
        pa = place("pa", 6, BT * S)
        pb = place("pb", 0, BT * S)
        pool_hi = place("pool_hi", 1, BT * S, F32R)
        pool_lo = place("pool_lo", 2, BT * S, F32R)
        mg_hi = place("mg_hi", 3, KT * S, F32R)
        mg_lo = place("mg_lo", 5, KT * S, F32R)
        res = place("res", 1, TOK * D)
        nf_row = place("nf_row", 0, D)
        hst = place("hst", 7, KT * S)
        diag = place("diag", 9.5, TOK * P)
        rstd_bc = place("rstd_bc", 9.75, 2 * S)
        PF = PASSES[0] * GROUP
        f_hi = place("f_hi", 3, PF * S, F32R)
        f_lo = place("f_lo", 6, PF * S, F32R)
        silu = place("silu", 9, GROUP * S)
        f32_ = place("f32_", 9.5, GROUP * S)
        y_out = place("y_out", 3, TOK * CHUNK)
        y_first = g1_row
        pu_first = g2_row

        bank = [ctx.enter_context(nc.psum_tensor(f"bank{i}", [P, 2 * 512], F32)) for i in range(4)]

        raw_full = [sem(f"raw_full{i}") for i in range(RING)]
        hi_done = sem("hi_done")
        lo_done = sem("lo_done")
        chunk_used = sem("chunk_used")
        pair_full = [sem(f"pair_full{i}") for i in range(MOD_RING)]
        mod_full = [sem(f"mod_full{i}") for i in range(MOD_RING)]
        mod_first = sem("mod_first")
        mod_used = sem("mod_used")
        side_done = {b: sem(f"side_done{b}") for b in (2, 3)}
        free = [sem(f"free{i}") for i in range(4)]
        par_in = sem("par_in")
        x_in = sem("x_in")
        gw_in = sem("gw_in")
        g2_in = sem("g2_in")
        rows_in = sem("rows_in")
        nf_in = sem("nf_in")
        res_in = sem("res_in")
        out_done = sem("out_done")
        ones_set = sem("ones_set")
        dve_order = sem("dve_order")
        silu_c_done = sem("silu_c_done")
        squared = sem("squared")
        sum_done = sem("sum_done")
        table_loaded = sem("table_loaded")
        root_done = sem("root_done")
        rstd1_done = sem("rstd1_done")
        normed_a = sem("normed_a")
        normed_b = sem("normed_b")
        turned = sem("turned")
        ahead = sem("ahead")
        diag_done = sem("diag_done")
        spread = sem("spread")
        neg_abs_done = sem("neg_abs_done")
        exp_done = sem("exp_done")
        softplus_done = sem("softplus_done")
        conv_done = sem("conv_done")
        tanh_done = sem("tanh_done")
        ixc_done = sem("ixc_done")
        sqrt_done = sem("sqrt_done")
        lru_f32 = sem("lru_f32")
        lru_high = sem("lru_high")
        lru_low = sem("lru_low")
        sc_f32 = sem("sc_f32")
        sc_high = sem("sc_high")
        sc_low = sem("sc_low")
        pool_f32 = sem("pool_f32")
        pool_high = sem("pool_high")
        pool_low = sem("pool_low")
        aff_done = sem("aff_done")
        res_scaled = sem("res_scaled")
        h_f32 = sem("h_f32")
        h_high = sem("h_high")
        h_low = sem("h_low")
        fin_done = sem("fin_done")
        mg_high = sem("mg_high")
        mg_low = sem("mg_low")
        f_high = sem("f_high")
        f_low = sem("f_low")
        res_done = sem("res_done")
        y_done = sem("y_done")
        rstd_done = sem("rstd_done")
        y_first_done = sem("y_first_done")

        def plus(const, step=0, i=0):
            return const + step * i if step else const

        block = ctx.enter_context(nc.Block())

        @block.sync
        def _(sync):
            def load(slot, chunk):
                return sync.dma_start(raw[slot][:, :], w_stream[chunk, :, :]).then_inc(raw_full[slot], 16)

            def load_mod(m):
                if m >= MOD_RING:
                    sync.wait_ge(mod_used, m - MOD_RING + 1)
                sync.dma_start(mod_raw[m % MOD_RING][:, :], m_stream[m, :, :]).then_inc(pair_full[m % MOD_RING], 16)

            sync.dma_start(par[:, :], params).then_inc(par_in, 16)
            chunk = 0
            for q in range(G_CHUNKS):
                for r in range(G_CHUNKS):
                    load_mod(q * G_CHUNKS + r)
                    if r == G_CHUNKS - 1 or (0 < q < G_CHUNKS - 1 and r in (2, 5)):
                        for _ in range({0: RING, G_CHUNKS - 1: 2}.get(q, 1)):
                            if chunk >= RING:
                                sync.wait_ge(lo_done, chunk - RING + 1)
                            load(chunk % RING, chunk)
                            chunk += 1
            assert chunk == PROJ
            with sync.Fori(PROJ // RING, N_CHUNKS // RING) as r:
                for c in range(RING):
                    sync.wait_ge(lo_done, 4 * r + (c - RING + 1))
                    sync.dma_start(raw[c][:, :],
                                   w_stream[bass.ds(4 * r + c, 1), :, :].rearrange("a p c -> p (a c)"))\
                        .then_inc(raw_full[c], 16)
            for t in range(TOK):
                sync.wait_ge(y_done, t + 1)
                sync.dma_start(out[t * P:(t + 1) * P, CHUNK:D], y_out[:, t * CHUNK:(t + 1) * CHUNK])\
                    .then_inc(out_done, 16)

        @block.gpsimd
        def _(pool):
            with pool.Fori(OPENING_MOD // MOD_RING, N_MOD // MOD_RING) as r:
                for c in range(MOD_RING):
                    pool.wait_ge(mod_used, 4 * r + (c - MOD_RING + 1))
                    pool.dma_start(mod_raw[c][:, :],
                                   m_stream[bass.ds(4 * r + c, 1), :, :].rearrange("a p c -> p (a c)"))\
                        .then_inc(mod_full[c], 16)

        @block.tensor
        def _(pe):
            def chunk_product(b, hi, lo, slot, k0, first_chunk, last_chunk):
                for kk in range(2):
                    act_hi, act_lo = (a[:, (k0 + kk) * S:(k0 + kk + 1) * S] for a in (hi, lo))
                    for m in range(GROUP):
                        acc = bank[b][:, m * S:(m + 1) * S]
                        cols = slice(kk * 512 + m * P, kk * 512 + (m + 1) * P)
                        first = first_chunk and kk == 0 and m % 2 == 0
                        nc.tensor.matmul(acc, w_hi[slot][:, cols], act_hi, start=first, stop=False,
                                         skip_group_check=True)
                        nc.tensor.matmul(acc, w_hi[slot][:, cols], act_lo, start=False, stop=False,
                                         skip_group_check=True)
                        mm = nc.tensor.matmul(acc, w_lo[slot][:, cols], act_hi, start=False,
                                              stop=last_chunk and kk == 1, skip_group_check=True)
                mm.then_inc(chunk_used, 1)

            def product(b, hi, lo, chunk, step, i, chunks, k0=0, ready=None):
                for c in range(chunks):
                    pe.wait_ge(lo_done, plus(chunk + c + 1, step, i))
                    if ready is not None:
                        pe.wait_ge(h_low, ready + c + 1)
                    chunk_product(b, hi, lo, (chunk + c) % RING, k0 + 2 * c, c == 0, c == chunks - 1)

            def wide(half, hi, lo, chunk, kts, uses, ready, midway=None):
                def tile(k, t, parts=(0, 1)):
                    b, slot = 2 * half + t, (chunk + k) % RING
                    if k == 0:
                        bank_free(b, uses[t])
                    cols = slice(k * S + t * P, k * S + (t + 1) * P)
                    for n, (act, w) in enumerate(((hi, w_hi), (hi, w_lo), (lo, w_hi))):
                        for q in parts:
                            mm = nc.tensor.matmul(bank[b][:, q * 512:(q + 1) * 512], act[:, cols],
                                                  w[slot][:, q * 512:(q + 1) * 512],
                                                  start=(k == 0 and n == 0), stop=(k == kts - 1 and n == 2))
                    return mm

                def stand(k):
                    pe.wait_ge(lo_done, chunk + k + 1)
                    if k % GROUP == 0:
                        pe.wait_ge(ready[0], ready[1] + k // GROUP + 1)

                for t in range(TOK):
                    for k in range(2):
                        if t == 0:
                            stand(k)
                        mm = tile(k, t)
                        if t:
                            mm.then_inc(chunk_used, 1)
                last = kts - RING if half else kts
                for k in range(2, last):
                    if k == kts // 2 and midway:
                        midway()
                    stand(k)
                    tile(k, 0)
                    tile(k, 1).then_inc(chunk_used, 1)
                if half:
                    for k in range(last, kts):
                        stand(k)
                        mm = tile(k, 0)
                    mm.then_inc(ahead, 1)
                    for k in range(last, kts):
                        mm = tile(k, 1, (0,))
                    mm.then_inc(ahead, 1)
                    for k in range(last, kts):
                        tile(k, 1, (1,)).then_inc(chunk_used, 1)

            def wides(task, hi, lo, chunk, kts, ready, midway=None):
                wide(0, hi, lo, chunk, kts, pe_acc, ready)
                wide(1, hi, lo, chunk + kts, kts, [side_use(task, b)[1] for b in (2, 3)], ready, midway)

            def bank_free(b, uses):
                if uses:
                    pe.wait_ge(free[b], uses)

            def mod_half(task, m, row):
                b, uses, _ = side_use(task)
                bank_free(b, uses)
                pe.wait_ge(mod_used, MOD_HALF * (m + 1))
                if row:
                    pe.wait_ge(ones_set, 1)
                for j in range(CHUNK // P if not row else 2):
                    if row:
                        mm = nc.tensor.matmul(bank[b][:, j * 512:(j + 1) * 512], ones[:, :],
                                              mod_acc[m % 2][:, j * 512:(j + 1) * 512], start=True, stop=True)
                    else:
                        mm = nc.tensor.transpose(bank[b][:, j * P:(j + 1) * P],
                                                 mod_acc[m % 2][:, j * P:(j + 1) * P], ident[:, :])
                mm.then_inc(side_done[b], 1)

            def turn(b, src, quarter, tiles=range(TOK)):
                for t in tiles:
                    for j in range(GROUP):
                        at = t * D + (quarter * GROUP + j) * P
                        mm = nc.tensor.transpose(bank[b][:, j * S + t * P:j * S + (t + 1) * P],
                                                 src[:, at:at + P], ident[:, :])
                return mm

            pe.wait_ge(par_in, 32)
            pe.wait_ge(normed_a, 1)
            pe.wait_ge(normed_b, 1)
            def turn_input(q):
                b, uses, _ = side_use(f"x{q}")
                bank_free(b, uses)
                turn(b, x_tok, q).then_inc(side_done[b], 1)

            turn_input(0)
            pe.wait_ge(ones_set, 1)
            groups = (0, 1, 3)
            for q in range(G_CHUNKS):
                b, uses, _ = side_use(f"s{q}")
                bank_free(b, uses)
                pe.wait_ge(mod_used, (q + 1) * G_CHUNKS)
                for j in range(GROUP):
                    for kk in range(2):
                        at = kk * 512 + j * P
                        mm = nc.tensor.matmul(bank[b][:, j:j + 1], mod_acc[q % 2][:, at:at + P], ones[:, 0:1],
                                              start=kk == 0, stop=kk == 1)
                mm.then_inc(side_done[b], 1)
                if q == 0:
                    for n in range(1, 4):
                        turn_input(n)
                pe.wait_ge(h_low, q + 1)
                for n, b in enumerate(groups):
                    chunk = q * OPENING + n
                    pe.wait_ge(lo_done, chunk + 1)
                    if q == 0 and b == 3:
                        bank_free(b, side_use("pool")[1])
                    chunk_product(b, h_hi, h_lo, chunk % RING, 2 * q, q == 0, q == G_CHUNKS - 1)

            pe_acc = [1, 1]
            for b in range(2):
                bank_free(b, 1)
                product(b, h_hi, h_lo, PROJ + b * G_CHUNKS, 0, 0, G_CHUNKS)
            pe_acc = [2, 2]

            pe.wait_ge(gw_in, 32)
            pe.wait_ge(conv_done, BT)
            for name, w in (("r", w_ga), ("i", w_gx)):
                for half in range(2):
                    b, uses, _ = side_use(f"{name}{half}")
                    bank_free(b, uses)
                    for j in range(GROUP):
                        t = half * GROUP + j
                        mm = nc.tensor.matmul(bank[b][:, j * S:(j + 1) * S], w[:, t * P:(t + 1) * P],
                                              xc[:, t * S:(t + 1) * S], start=True, stop=True)
                    mm.then_inc(side_done[b], 1)

            with pe.Fori(0, A_GROUPS // 2 - 2) as i:
                for b in range(2):
                    pe.wait_ge(free[b], plus(pe_acc[b], 1, i))
                    product(b, h_hi, h_lo, PROJ + (2 + b) * G_CHUNKS, 2 * G_CHUNKS, i, G_CHUNKS)
            pe_acc = [n + A_GROUPS // 2 - 2 for n in pe_acc]
            mod_half("m4", 4, row=True)
            mod_half("m5", 5, row=True)

            def branch(chunk0, acts, ready, parts=1):
                with pe.Fori(0, 4) as i:
                    pe.wait_ge(free[0], plus(pe_acc[0], 1, i))
                    product(0, h_hi, h_lo, chunk0, PAIR, i, G_CHUNKS)
                    pe.wait_ge(free[1], plus(pe_acc[1], 1, i))
                    pe.wait_ge(ready, parts)
                    product(1, *acts, chunk0 + G_CHUNKS, PAIR, i, OUT_CHUNKS)
                return [n + 4 for n in pe_acc]

            pe_acc = branch(LRU_OUT, (lru_hi, lru_lo), lru_low)
            mod_half("m6", 6, row=False)
            mod_half("m7", 7, row=False)

            bank_free(1, pe_acc[1])
            product(1, h_hi, h_lo, POOL_IN, 0, 0, G_CHUNKS)
            pe_acc[1] += 1
            pe_acc = branch(SC_OUT, (sc_hi, sc_lo), sc_low, 2)
            mod_half("m8", 8, row=False)
            mod_half("m9", 9, row=False)

            for j in range(4):
                bank_free(0, pe_acc[0])
                product(0, h_hi, h_lo, POOL_OUT + j * POOL_PAIR, 0, 0, G_CHUNKS)
                bank_free(1, pe_acc[1])
                pe.wait_ge(pool_low, 1)
                product(1, pool_hi, pool_lo, POOL_OUT + j * POOL_PAIR + G_CHUNKS, 0, 0, 1, k0=2 * j)
                pe_acc = [n + 1 for n in pe_acc]

            def turn_first_half():
                pe.wait_ge(res_done, TOK)
                for q in range(2):
                    turn(q, res, q).then_inc(turned, 1)

            wides("wide_o", mg_hi, mg_lo, W_O, KT, (mg_low, 0), turn_first_half)
            pe_acc = [n + 2 for n in pe_acc]

            def spread_rstd(t):
                pe.wait_ge(diag_done, t + 1)
                for n in range(2):
                    mm = nc.tensor.matmul(bank[0][:, n * S + t * P:n * S + (t + 1) * P], ones[:, :],
                                          diag[:, t * P:(t + 1) * P], start=True, stop=True)
                mm.then_inc(spread, 1)

            pe.wait_ge(res_done, TOK + 1)
            turn(2, res, 2, (0,))
            bank_free(0, pe_acc[0])
            spread_rstd(0)
            bank_free(3, side_use("turn3")[1])
            turn(3, res, 3, (0,))
            for q in (2, 3):
                pe.wait_ge(res_done, TOK + q)
                turn(q, res, q, (1,)).then_inc(turned, 1)
            spread_rstd(1)
            pe_acc[0] += 1

            for p, groups in enumerate(PASSES):
                up, down = FFN[p]
                with pe.Fori(0, groups) as i:
                    for b in range(2):
                        pe.wait_ge(free[b], plus(pe_acc[b], 1, i))
                        product(b, h_hi, h_lo, up + b * G_CHUNKS, 2 * G_CHUNKS, i, G_CHUNKS,
                                ready=G_CHUNKS)
                pe_acc = [n + groups for n in pe_acc]
                if p == 0:
                    mod_half("m10", 10, row=True)
                    mod_half("m11", 11, row=True)
                wides(f"wide_f{p}", f_hi, f_lo, down, groups * GROUP, (f_low, sum(PASSES[:p])))
                pe_acc = [n + 1 for n in pe_acc]

        @block.scalar
        def _(act):
            act.dma_start(ident[:, :], ident_in).then_inc(par_in, 16)
            for t in range(TOK):
                act.dma_start(x_tok[:, t * D:(t + 1) * D], x[t * P:(t + 1) * P, :]).then_inc(x_in, 16)

            def high(chunk, step=0, i=0, n=1):
                for c in range(chunk, chunk + n):
                    if c >= N_CHUNKS:
                        return
                    act.wait_ge(raw_full[c % RING], plus(16 * (c // RING + 1), 16 * step // RING, i))
                    if c >= RING:
                        act.wait_ge(chunk_used, plus(c - RING + 1, step, i))
                    nc.scalar.activation(w_hi[c % RING][:, :], raw[c % RING][:, :], ACT.Copy).then_inc(hi_done, 1)

            act.wait_ge(par_in, 32)
            nc.scalar.activation(silu_c[:, :], par[:, P_C:P_C + KT], ACT.Silu).then_inc(silu_c_done, 1)
            act.wait_ge(neg_abs_done, 1)
            nc.scalar.activation(sp[:, BT:2 * BT], sp[:, 0:BT], ACT.Exp).then_inc(exp_done, 1)
            act.wait_ge(x_in, 32)
            act.wait_ge(ones_set, 1)

            def squares(junk, src, to, before):
                if before:
                    act.wait_ge(squared, before)
                nc.scalar.activation(junk, src, ACT.Square, accum_out=stat[:, to:to + 1]).then_inc(squared, 1)

            def root(src, to):
                nc.scalar.activation(stat[:, to], stat[:, src], ACT.Sqrt, bias=eps[:, 0:1], scale=1.0 / D)\
                    .then_inc(root_done, 1)

            for t in range(TOK):
                squares(sq_junk[:, :], x_tok[:, t * D:(t + 1) * D], t, t)
            act.wait_ge(squared, TOK)
            root(slice(0, 2), slice(2, 4))

            def take_input(q):
                b, _, done = side_use(f"x{q}")
                act.wait_ge(side_done[b], done)
                nc.scalar.activation(xn[:, q * CHUNK:(q + 1) * CHUNK], bank[b][:, :], ACT.Copy).then_inc(free[b], 1)

            def modulate(src, q, scale, shift):
                for n in range(2):
                    part = src[:, (2 * q + n) * S:(2 * q + n + 1) * S]
                    ins = nc.scalar.activation(part, part, ACT.Identity, scale=scale[:, n:n + 1],
                                               bias=shift[:, n:n + 1])
                ins.then_inc(h_f32, 1)

            def h_high_part(src, q, before):
                act.wait_ge(h_f32, before + 1)
                nc.scalar.activation(h_hi[:, q * 512:(q + 1) * 512], src[:, q * 512:(q + 1) * 512],
                                     ACT.Copy).then_inc(h_high, 1)

            act.wait_ge(rstd1_done, 1)
            nc.scalar.activation(x_tok[:, D:2 * D], x_tok[:, D:2 * D], ACT.Copy, scale=stat[:, 3:4])\
                .then_inc(normed_b, 1)
            take_input(0)
            high(0, n=OPENING)
            for q in range(G_CHUNKS):
                high((q + 1) * OPENING - 2 * (q == G_CHUNKS - 1))
                if q % 2 == 0:
                    b, uses, _ = side_use(f"x{q // 2}")
                    act.wait_ge(free[b], uses + 1)
                act.wait_ge(aff_done, q + 1)
                modulate(xn, q, aff[:, 2 * q:2 * q + 2], modc[:, 4 * q + 2:4 * q + 4])
                h_high_part(xn, q, q)
                if q == 0:
                    for n in range(1, 4):
                        take_input(n)
                if q < G_CHUNKS - 2:
                    high((q + 1) * OPENING + 1, n=OPENING - 1)
            high(PROJ - 1)
            act.dma_start(w_ga[:, :], gate_w[0]).then_inc(gw_in, 16)
            act.dma_start(w_gx[:, :], gate_w[1]).then_inc(gw_in, 16)
            act.dma_start(g1_row[:, :], rows[0:1, :].to_broadcast([P, D])).then_inc(rows_in, 16)
            act.dma_start(cnt[:, :], pool_cnt).then_inc(rows_in, 16)

            def take(dst, half, b, end, func=ACT.Copy):
                act.wait_ge(chunk_used, end)
                nc.scalar.activation(dst[:, half * CHUNK:(half + 1) * CHUNK], bank[b][:, :], func)\
                    .then_inc(free[b], 1)

            high(PROJ)
            for b in range(2):
                high(PROJ + 1 + b)
                take(lx, b, b, PROJ - OPENING + b + 1)
            high(PROJ + OPENING)
            take(pu_first, 0, 3, PROJ)

            def r_or_i(name, dst, bias):
                for half in range(2):
                    b, _, done = side_use(f"{name}{half}")
                    act.wait_ge(side_done[b], done)
                    for j in range(GROUP):
                        t = half * GROUP + j
                        ins = nc.scalar.activation(dst[:, t * S:(t + 1) * S], bank[b][:, j * S:(j + 1) * S],
                                                   ACT.Sigmoid, bias=par[:, bias + t:bias + t + 1])
                    ins.then_inc(free[b], 1)

            targets = [lx, lg, sb_, sc_]
            for g in range(2, A_GROUPS):
                high(PROJ + (g - 2) * G_CHUNKS + RING, n=G_CHUNKS)
                if g < 8:
                    take(targets[g // 2], g % 2, g % 2, PROJ + (g - 1) * G_CHUNKS,
                         ACT.Gelu_apprx_tanh if g // 2 == 1 else ACT.Copy)
                if g == 3:
                    r_or_i("r", lr, P_BA)
                    r_or_i("i", li, P_BX)
                    act.wait_ge(softplus_done, 1)
                    b, uses, _ = side_use("r1")
                    act.wait_ge(free[b], uses + 1)
                    for t in range(BT):
                        ins = nc.scalar.activation(lr[:, t * S:(t + 1) * S], lr[:, t * S:(t + 1) * S], ACT.Tanh,
                                                   scale=sp[:, 7 * BT + t:7 * BT + t + 1])
                    ins.then_inc(tanh_done, 1)
                    act.wait_ge(tanh_done, 1)
                if g == 4:
                    act.wait_ge(ixc_done, 1)
                    nc.scalar.activation(xc[:, :], lr[:, :], ACT.Sqrt).then_inc(sqrt_done, 1)
                if g == 7:
                    act.wait_ge(lru_f32, 1)
                    nc.scalar.activation(lru_hi[:, :], lg[:, :], ACT.Copy).then_inc(lru_high, 1)

            uses = [A_GROUPS // 2] * 2

            def sigmoid_gates(chunk_end, step, i, merged_before):
                act.wait_ge(chunk_used, plus(chunk_end, step, i))
                act.wait_ge(free[1], plus(merged_before, 1 if step else 0, i))
                nc.scalar.activation(gate[:, :], bank[0][:, :], ACT.Sigmoid).then_inc(free[0], 1)

            def gates(chunk0, merged_before):
                with act.Fori(0, 4) as i:
                    high(chunk0 + RING, PAIR, i, G_CHUNKS)
                    sigmoid_gates(chunk0 + G_CHUNKS, PAIR, i, merged_before)
                    high(chunk0 + RING + G_CHUNKS, PAIR, i, OUT_CHUNKS)

            gates(LRU_OUT, uses[1])
            uses = [n + 4 for n in uses]
            high(POOL_IN + RING, n=2)
            act.wait_ge(sc_f32, 1)
            nc.scalar.activation(sc_hi[:, :], sv[:, :], ACT.Copy).then_inc(sc_high, 1)
            high(POOL_IN + RING + 2, n=G_CHUNKS - 2)
            take(pu, 1, 1, POOL_IN + G_CHUNKS)
            uses[1] += 1
            gates(SC_OUT, uses[1])
            uses = [n + 4 for n in uses]
            act.wait_ge(pool_f32, 1)
            nc.scalar.activation(pool_hi[:, :], pa[:, :], ACT.Copy).then_inc(pool_high, 1)
            for j in range(4):
                chunk = POOL_OUT + j * POOL_PAIR
                high(chunk + RING, n=G_CHUNKS)
                sigmoid_gates(chunk + G_CHUNKS, 0, 0, uses[1] + j)
                high(chunk + RING + G_CHUNKS)
                if j == 1:
                    act.dma_start(g2_row[:, :], rows[1:2, :].to_broadcast([P, D])).then_inc(g2_in, 16)
                if j == 2:
                    act.dma_start(nf_row[:, :], rows[2:3, :].to_broadcast([P, D])).then_inc(nf_in, 16)
                act.wait_ge(fin_done, j + 1)
                nc.scalar.activation(mg_hi[:, j * CHUNK:(j + 1) * CHUNK], merged[:, j * CHUNK:(j + 1) * CHUNK],
                                     ACT.Copy).then_inc(mg_high, 1)
            uses = [n + 4 for n in uses]
            for t in range(TOK):
                high(W_O + (t + 1) * RING, n=RING)
                act.dma_start(res[:, t * D:(t + 1) * D], x[t * P:(t + 1) * P, :]).then_inc(res_in, 16)

            def part_squares(n, norm):
                t, at, width = ((0, 0, CHUNK), (1, 0, CHUNK), (0, CHUNK, CHUNK), (1, CHUNK, 512),
                                (1, CHUNK + 512, 512))[n]
                done = (norm - 2) * 5 + n
                act.wait_ge(res_done, done + 1)
                squares(silu[:, 0:width], res[:, t * D + at:t * D + at + width], 4 + (norm - 2) * 9 + n, TOK + done)

            def table_of_roots():
                nc.scalar.activation(no_use[:, :], eps[:, :], ACT.Sqrt).then_inc(table_loaded, 1)

            def tile_root(t, norm):
                act.wait_ge(sum_done, (norm - 2) * TOK + t + 1)
                at = 9 + (norm - 2) * 9 + t
                root(slice(at, at + 1), slice(at + 2, at + 3))

            high(W_O + (TOK + 1) * RING, n=HALF_O + RING - TOK * RING)
            for n in range(2):
                part_squares(n, 2)
            mid, end = W_O + HALF_O, W_O + 2 * HALF_O
            high(mid + 2 * RING, n=HALF_O // 2 - RING + 1)
            for q in range(2):
                act.wait_ge(turned, q + 1)
                nc.scalar.activation(hst[:, q * CHUNK:(q + 1) * CHUNK], bank[q][:, :], ACT.Copy).then_inc(free[q], 1)
            high(mid + HALF_O // 2 + RING + 1, n=HALF_O // 2 - RING - 1)
            table_of_roots()
            part_squares(2, 2)
            tile_root(0, 2)
            part_squares(3, 2)
            high(end, n=RING - 2)
            part_squares(4, 2)
            tile_root(1, 2)
            high(end + RING - 2, n=2)
            for q in range(G_CHUNKS):
                if q in (5, 7):
                    b = q // 2
                    act.wait_ge(free[b], side_use(f"turn{b}")[1] + 1)
                else:
                    act.wait_ge(res_scaled, q + 1 - (q > 5))
                modulate(hst, q, aff[:, KT + 2 * q:], aff[:, 2 * KT + 2 * q:])
                h_high_part(hst, q, G_CHUNKS + q)
                if q >= 4:
                    high(FFN[0][0] + RING + q - 4)
            uses = [uses[0] + 3, uses[1] + 2]

            for p, groups in enumerate(PASSES):
                up, down = FFN[p]
                before = sum(PASSES[:p])

                def hidden(i, fed=0):
                    high(up + RING + fed, 2 * G_CHUNKS, i, G_CHUNKS - fed)
                    act.wait_ge(chunk_used, plus(up + G_CHUNKS, 2 * G_CHUNKS, i))
                    act.wait_ge(free[1], plus(uses[1], 1, i))
                    nc.scalar.activation(silu[:, :], bank[0][:, :], ACT.Silu).then_inc(free[0], 1)
                    high(up + RING + G_CHUNKS, 2 * G_CHUNKS, i, G_CHUNKS)
                    act.wait_ge(free[1], plus(uses[1] + 1, 1, i))
                    nc.scalar.activation(f_hi[:, bass.ds(i * CHUNK, CHUNK)], f32_[:, :], ACT.Copy)\
                        .then_inc(f_high, 1)

                if p == 0:
                    hidden(0, 4)
                with act.Fori(int(p == 0), groups) as i:
                    hidden(i)
                uses = [n + groups + 1 for n in uses]
                half = groups * GROUP
                high(down + RING, n=half + RING)
                if p:
                    for n in range(2):
                        part_squares(n, 3)
                high(down + half + 2 * RING, n=half - RING)

            act.wait_ge(table_loaded, 1)
            table_of_roots()
            for t in range(TOK):
                for n in ((2,), (3, 4))[t]:
                    part_squares(n, 3)
                tile_root(t, 3)
                act.wait_ge(rstd_done, t + 1)
                part = y_first[:, t * CHUNK:(t + 1) * CHUNK]
                nc.scalar.activation(part, part, ACT.Copy, scale=stat[:, 20 + t:21 + t]).then_inc(y_first_done, 1)
                act.wait_ge(y_first_done, t + 1)
                act.dma_start(out[t * P:(t + 1) * P, 0:CHUNK], part).then_inc(out_done, 16)
            act.wait_ge(out_done, 32 * TOK)

        @block.vector
        def _(dve):
            def step(ins, done=dve_order):
                ins.then_inc(done, 1)
                stood[done.name] = stood.get(done.name, 0) + 1
                dve.wait_ge(done, stood[done.name])

            stood = {}
            V = nc.vector

            def low(chunk, stride=0, i=0, n=1):
                for c in range(chunk, chunk + n):
                    if c >= N_CHUNKS:
                        return
                    dve.wait_ge(hi_done, plus(c + 1, stride, i))
                    V.tensor_tensor(w_lo[c % RING][:, :], raw[c % RING][:, :], w_hi[c % RING][:, :].bitcast(F32),
                                    ALU.subtract).then_inc(lo_done, 1)

            def half_reduced(m):
                b, _, done = side_use(f"m{m}" if m >= 4 else f"s{m + G_CHUNKS - 4}")
                dve.wait_ge(side_done[b], done)

            def mod(m, n=1):
                for c in range(m, m + n):
                    k, acc = c % MOD_HALF, mod_acc[(c // MOD_HALF) % 2]
                    dve.wait_ge(mod_full[c % MOD_RING], 16 * ((c - OPENING_MOD) // MOD_RING + 1))
                    if k == 0:
                        half_reduced(c // MOD_HALF - 2)
                        V.tensor_scalar(acc[:, :], mod_raw[c % MOD_RING][:, :], silu_c[:, 0:1], None,
                                        ALU.mult).then_inc(mod_used, 1)
                    else:
                        dve.wait_ge(mod_used, c)
                        V.scalar_tensor_tensor(out=acc[:, :], in0=mod_raw[c % MOD_RING][:, :],
                                               scalar=silu_c[:, k:k + 1], in1=acc[:, :],
                                               op0=ALU.mult, op1=ALU.add).then_inc(mod_used, 1)

            def sums(task, dst, at):
                b, uses, done = side_use(task)
                dve.wait_ge(side_done[b], done)
                V.tensor_reduce(dst[:, at:at + CHUNK // P], bank[b][:, :].rearrange("p (j k) -> p j k", k=P),
                                AX.X, ALU.add).then_inc(free[b], 1)
                dve.wait_ge(free[b], uses + 1)

            def row_sums(task, dst, half):
                b, uses, done = side_use(task)
                dve.wait_ge(side_done[b], done)
                cols = slice(half * CHUNK, (half + 1) * CHUNK)
                V.tensor_tensor(dst[:, cols], bank[b][:, :], dst[:, cols], ALU.add).then_inc(free[b], 1)
                dve.wait_ge(free[b], uses + 1)

            def affine(sc_at, sh_at, b_sc, b_sh, norm, to):
                step(V.tensor_tensor(modc[:, sc_at:sc_at + KT], modc[:, sc_at:sc_at + KT],
                                     par[:, P_BMOD + b_sc * KT:P_BMOD + (b_sc + 1) * KT], ALU.add))
                step(V.scalar_tensor_tensor(out=aff[:, to:to + KT], in0=modc[:, sc_at:sc_at + KT], scalar=1.0,
                                            in1=par[:, norm:norm + KT], op0=ALU.add, op1=ALU.mult))
                step(V.tensor_tensor(aff[:, to + KT:to + 2 * KT], modc[:, sh_at:sh_at + KT],
                                     par[:, P_BMOD + b_sh * KT:P_BMOD + (b_sh + 1) * KT], ALU.add))

            V.memset(eps[:, :], EPS).then_inc(dve_order, 1)
            V.memset(ones[:, :], 1.0).then_inc(ones_set, 1)
            stood[dve_order.name] = 1
            dve.wait_ge(dve_order, 1)
            dve.wait_ge(ones_set, 1)
            dve.wait_ge(par_in, 32)
            lam = par[:, P_LAM:P_LAM + BT]

            def spc(i):
                return sp[:, i * BT:(i + 1) * BT]

            step(V.tensor_scalar(spc(2), lam, -1.0, 0.0, ALU.mult, ALU.max))
            step(V.scalar_tensor_tensor(out=spc(0), in0=spc(2), scalar=-2.0, in1=lam, op0=ALU.mult,
                                        op1=ALU.subtract), neg_abs_done)

            def mod_pair(q, r):
                m = q * G_CHUNKS + r
                acc, src = mod_acc[q % 2], mod_raw[m % MOD_RING]
                dve.wait_ge(pair_full[m % MOD_RING], 16 * (m // MOD_RING + 1))
                if r == 0 and q >= 2:
                    b, _, done = side_use(f"s{q - 2}")
                    dve.wait_ge(side_done[b], done)
                if r == 0 and q < 2:
                    dve.wait_ge(silu_c_done, 1)
                for kk in range(2):
                    if r:
                        dve.wait_ge((mod_first, mod_used)[kk], m)
                    k, cols = 2 * r + kk, slice(kk * 512, (kk + 1) * 512)
                    if r == 0:
                        ins = V.tensor_scalar(acc[:, cols], src[:, cols], silu_c[:, k:k + 1], None, ALU.mult)
                    else:
                        ins = V.scalar_tensor_tensor(out=acc[:, cols], in0=src[:, cols], scalar=silu_c[:, k:k + 1],
                                                     in1=acc[:, cols], op0=ALU.mult, op1=ALU.add)
                    ins.then_inc((mod_first, mod_used)[kk], 1)

            for r in range(6):
                mod_pair(0, r)
            dve.wait_ge(root_done, 1)
            step(V.reciprocal(stat[:, 2:4], stat[:, 2:4]), rstd1_done)
            V.tensor_scalar(x_tok[:, 0:D], x_tok[:, 0:D], stat[:, 2:3], None, ALU.mult).then_inc(normed_a, 1)
            for r in range(6, G_CHUNKS):
                mod_pair(0, r)
            def h_pair(q):
                b, uses, done = side_use(f"s{q}")
                both, k = modc[:, 4 * q:4 * q + 4], 2 * q
                dve.wait_ge(side_done[b], done)
                V.tensor_tensor(both, bank[b][:, 0:4], par[:, P_B1 + 4 * q:P_B1 + 4 * q + 4], ALU.add)\
                    .then_inc(free[b], 1)
                dve.wait_ge(free[b], uses + 1)
                step(V.scalar_tensor_tensor(out=aff[:, k:k + 2], in0=both[:, 0:2], scalar=1.0,
                                            in1=par[:, P_NMIX + k:P_NMIX + k + 2], op0=ALU.add, op1=ALU.mult),
                     aff_done)

            def h_low_part(src, q, before):
                dve.wait_ge(h_high, before + 1)
                V.tensor_tensor(h_lo[:, q * 512:(q + 1) * 512], src[:, q * 512:(q + 1) * 512],
                                h_hi[:, q * 512:(q + 1) * 512].bitcast(F32), ALU.subtract).then_inc(h_low, 1)

            low(0, n=OPENING)
            for q in range(G_CHUNKS):
                following = iter(range(G_CHUNKS)) if q + 1 < G_CHUNKS else iter(())

                def next_mod(n):
                    for _, r in zip(range(n), following):
                        mod_pair(q + 1, r)

                next_mod(1)
                h_pair(q)
                low((q + 1) * OPENING - 2 * (q == G_CHUNKS - 1))
                next_mod(1)
                h_low_part(xn, q, q)
                for c, n in ((1, 4), (2, 2)):
                    next_mod(n)
                    if q < G_CHUNKS - 2:
                        low((q + 1) * OPENING + c)
            low(PROJ - 1)
            dve.wait_ge(exp_done, 1)
            step(V.tensor_scalar(spc(3), spc(1), 2.0, None, ALU.add))
            step(V.reciprocal(spc(3), spc(3)))
            step(V.tensor_tensor(spc(3), spc(3), spc(1), ALU.mult))
            step(V.tensor_tensor(spc(4), spc(3), spc(3), ALU.mult))
            step(V.memset(spc(5), 1.0 / 17))
            for n in range(15, 0, -2):
                step(V.tensor_tensor(spc(5), spc(5), spc(4), ALU.mult))
                step(V.tensor_scalar(spc(5), spc(5), 1.0 / n, None, ALU.add))
            step(V.tensor_tensor(spc(5), spc(5), spc(3), ALU.mult))
            step(V.scalar_tensor_tensor(out=spc(6), in0=spc(5), scalar=2.0, in1=spc(2), op0=ALU.mult, op1=ALU.add))
            step(V.tensor_scalar(spc(7), spc(6), 4.0, None, ALU.mult), softplus_done)
            low(PROJ, n=RING)

            def three_d(t):
                return t[:, :].rearrange("p (j s) -> p j s", s=S)

            def conv(dst, src, tiles, taps, width, bias=None, done=dve_order):
                for t in tiles:
                    o, u = t * S, (t + 1) * S
                    w = taps + (width - 1) * BT + t
                    if bias is None:
                        step(V.tensor_scalar(dst[:, o:u], src[:, o:u], par[:, w:w + 1], None, ALU.mult))
                    else:
                        step(V.tensor_scalar(dst[:, o:u], src[:, o:u], par[:, w:w + 1],
                                             par[:, bias + t:bias + t + 1], ALU.mult, ALU.add))
                    for back in range(1, width):
                        w = taps + (width - 1 - back) * BT + t
                        step(V.scalar_tensor_tensor(out=dst[:, o + back:u], in0=src[:, o:u - back],
                                                    scalar=par[:, w:w + 1], in1=dst[:, o + back:u],
                                                    op0=ALU.mult, op1=ALU.add),
                             done if back == width - 1 else dve_order)

            mods = [0, 0, 3, 3, 6, 1, 2, 7, 6, 4]
            m, t_conv = OPENING_MOD, 0
            for b in range(2):
                dve.wait_ge(free[b], 1)
            for g in range(2, A_GROUPS):
                for c in range(G_CHUNKS):
                    low(PROJ + (g - 2) * G_CHUNKS + RING + c)
                    if c * mods[g] % G_CHUNKS < mods[g]:
                        mod(m)
                        m += 1
                    if t_conv < BT and (g == 2 and c % 2 == 0 or g == 3 and c < 4):
                        conv(xc, lx, (t_conv,), P_CONVW, 4, P_CONVB, conv_done)
                        t_conv += 1
                    if g == 4 and c == 4:
                        dve.wait_ge(tanh_done, 1)
                        step(V.tensor_tensor(li[:, :], li[:, :], xc[:, :], ALU.mult), ixc_done)
                    if g == 4 and c == 6:
                        step(V.tensor_scalar(lx[:, :], lr[:, :], 1.0, None, ALU.add))
                    if g == 5:
                        part = lx[:, c * S:(c + 1) * S]
                        step(V.reciprocal(part, part))
                    half = slice(c % 2 * CHUNK, (c % 2 + 1) * CHUNK)
                    if g == 6 and c < 2:
                        dve.wait_ge(sqrt_done, 1)
                        step(V.scalar_tensor_tensor(out=xc[:, half], in0=xc[:, half], scalar=2.0, in1=lx[:, half],
                                                    op0=ALU.mult, op1=ALU.mult))
                    if g == 6 and c == 2:
                        step(V.memset(three_d(xc)[:, :, 0:1], 1.0))
                    if g == 6 and c in (2, 3):
                        step(V.tensor_tensor(li[:, half], li[:, half], xc[:, half], ALU.mult))
                    if g == 6 and c == 4:
                        step(V.tensor_scalar(lr[:, :], lr[:, :], -1.0, 1.0, ALU.mult, ALU.add))
                    if g == 6 and c >= 6:
                        step(V.tensor_tensor(lr[:, half], lr[:, half], lx[:, half], ALU.mult))
                    if g == 6 and c == 7:
                        step(V.memset(three_d(lr)[:, :, 0:1], 0.0))
                    if g == 7 and c == 0:
                        step(V.tensor_tensor_scan(lx[:, :], lr[:, :], li[:, :], 0.0, ALU.mult, ALU.add))
                    if g == 7 and c == 4:
                        step(V.tensor_tensor(lg[:, :], lg[:, :], lx[:, :], ALU.mult), lru_f32)
                    if g == 8 and c == 4:
                        dve.wait_ge(lru_high, 1)
                        step(V.tensor_tensor(lru_lo[:, :], lg[:, :], lru_hi[:, :].bitcast(F32), ALU.subtract),
                             lru_low)
                if g >= 8:
                    b = g % 2
                    cols = slice(b * CHUNK, (b + 1) * CHUNK)
                    dve.wait_ge(chunk_used, PROJ + (g - 1) * G_CHUNKS)
                    V.tensor_tensor(sc_[:, cols], bank[b][:, :], sc_[:, cols], ALU.mult).then_inc(free[b], 1)
            dve.wait_ge(rows_in, 32)
            row_sums("m4", g1_row, 0)
            row_sums("m5", g1_row, 1)

            def merge(j, uses, branch_no, chunk_end):
                dst = merged[:, j * CHUNK:(j + 1) * CHUNK]
                dve.wait_ge(free[0], uses[0] + j + 1)
                dve.wait_ge(chunk_used, chunk_end)
                if branch_no == 0:
                    V.tensor_tensor(dst, bank[1][:, :], gate[:, :], ALU.mult).then_inc(free[1], 1)
                    return
                if branch_no == 1:
                    V.tensor_tensor(term[:, :], bank[1][:, :], gate[:, :], ALU.mult).then_inc(free[1], 1)
                else:
                    for m in range(GROUP):
                        cols = slice(m * S, (m + 1) * S)
                        at = P_PSCALE + j * GROUP + m
                        ins = V.scalar_tensor_tensor(out=term[:, cols], in0=bank[1][:, cols],
                                                     scalar=par[:, at:at + 1], in1=gate[:, cols],
                                                     op0=ALU.mult, op1=ALU.mult)
                    ins.then_inc(free[1], 1)
                dve.wait_ge(free[1], uses[1] + j + 1)
                step(V.tensor_tensor(dst, dst, term[:, :], ALU.add), fin_done if branch_no == 2 else dve_order)

            uses = [A_GROUPS // 2] * 2
            for j in range(4):
                for c in range(PAIR - 1):
                    low(LRU_OUT + j * PAIR + RING + c)
                    if c < 8:
                        mod(96 + 8 * j + c)
                    if c in (9, 10):
                        conv(sv, sc_, (2 * j + c - 9,), P_SCW, 3)
                merge(j, uses, 0, LRU_OUT + (j + 1) * PAIR)
                low(LRU_OUT + (j + 1) * PAIR + RING - 1)
            uses = [n + 4 for n in uses]
            sums("m6", modc, 2 * KT)
            sums("m7", modc, 2 * KT + CHUNK // P)
            step(V.tensor_tensor(sv[:, :], sv[:, :], sb_[:, :], ALU.mult), sc_f32)
            low(POOL_IN + RING, n=4)
            dve.wait_ge(sc_high, 1)
            for half in range(2):
                cols = slice(half * CHUNK, (half + 1) * CHUNK)
                step(V.tensor_tensor(sc_lo[:, cols], sv[:, cols], sc_hi[:, cols].bitcast(F32), ALU.subtract), sc_low)
                low(POOL_IN + RING + 4 + half)
            low(POOL_IN + RING + 6, n=G_CHUNKS - 6)
            uses[1] += 1

            def pool_means():
                tiles = BT // 4
                for g, window in enumerate(POOL_WINDOWS):
                    cols = slice(g * tiles * S, (g + 1) * tiles * S)
                    u = pu_first if g < 2 else pu
                    src, w = u, 1
                    for dst in (pa, pb, pa, pb)[:g + 1]:
                        s3 = src[:, cols].rearrange("p (j s) -> p j s", s=S)
                        d3 = dst[:, cols].rearrange("p (j s) -> p j s", s=S)
                        step(V.tensor_tensor(d3[:, :, w:], s3[:, :, w:], s3[:, :, :S - w], ALU.add))
                        step(V.tensor_copy(d3[:, :, 0:w], s3[:, :, 0:w]))
                        src, w = dst, 2 * w
                    dst = pa
                    s3 = src[:, cols].rearrange("p (j s) -> p j s", s=S)
                    at = sum(POOL_WINDOWS[:g])
                    for j in range(tiles):
                        step(V.tensor_tensor(s3[:, j, 0:window], s3[:, j, 0:window], cnt[:, at:at + window],
                                             ALU.mult))
                    step(V.scalar_tensor_tensor(out=dst[:, cols], in0=src[:, cols], scalar=1.0 / window,
                                                in1=u[:, cols], op0=ALU.mult, op1=ALU.subtract),
                         pool_f32 if g == 3 else dve_order)
                    yield

            dve.wait_ge(free[1], uses[1])
            dve.wait_ge(free[3], side_use("pool")[1] + 1)
            pooling = pool_means()
            for j in range(4):
                for c in range(PAIR - 1):
                    low(SC_OUT + j * PAIR + RING + c)
                    if c < 8:
                        mod(128 + 8 * j + c)
                    if c == 9:
                        next(pooling)
                merge(j, uses, 1, SC_OUT + (j + 1) * PAIR)
                low(SC_OUT + (j + 1) * PAIR + RING - 1)
            uses = [n + 4 for n in uses]
            sums("m8", modc, 3 * KT)
            sums("m9", modc, 3 * KT + CHUNK // P)
            affine(3 * KT, 2 * KT, 4, 3, P_NFFN, KT)

            low(POOL_OUT + RING)
            dve.wait_ge(pool_high, 1)
            step(V.tensor_tensor(pool_lo[:, :], pa[:, :], pool_hi[:, :].bitcast(F32), ALU.subtract), pool_low)
            for j in range(4):
                low(POOL_OUT + j * POOL_PAIR + RING + (j == 0), n=POOL_PAIR - 1 - (j == 0))
                merge(j, uses, 2, POOL_OUT + (j + 1) * POOL_PAIR)
                low(POOL_OUT + (j + 1) * POOL_PAIR + RING - 1)
                dve.wait_ge(mg_high, j + 1)
                V.tensor_tensor(mg_lo[:, j * CHUNK:(j + 1) * CHUNK], merged[:, j * CHUNK:(j + 1) * CHUNK],
                                mg_hi[:, j * CHUNK:(j + 1) * CHUNK].bitcast(F32), ALU.subtract).then_inc(mg_low, 1)
            uses = [n + 4 for n in uses]

            def row_sum(t, norm):
                at = 4 + (norm - 2) * 9
                dve.wait_ge(squared, TOK + (norm - 2) * 5 + (3, 5)[t])
                col = [stat[:, at + n:at + n + 1] for n in range(8)]
                if t == 0:
                    step(V.tensor_tensor(col[5], col[0], col[2], ALU.add), sum_done)
                else:
                    step(V.scalar_tensor_tensor(out=col[6], in0=col[1], scalar=col[3], in1=col[4], op0=ALU.add,
                                                op1=ALU.add), sum_done)

            def root_of(t, norm):
                dve.wait_ge(root_done, (norm - 2) * TOK + t + 2)
                at = 11 + (norm - 2) * 9 + t
                return stat[:, at:at + 1]

            def update(half, t, g_row, before, done, final=False, part=None):
                b = 2 * half + t
                cols = slice(0, CHUNK) if part is None else slice(part * 512, (part + 1) * 512)
                width, at = cols.stop - cols.start, half * CHUNK + cols.start
                old = res[:, t * D + at:t * D + at + width]
                new = mod_acc[t][:, cols]
                ins = V.tensor_tensor(new, bank[b][:, cols], g_row[:, at:at + width], ALU.mult)
                if part == 0:
                    step(ins)
                else:
                    ins.then_inc(free[b], 1)
                    dve.wait_ge(free[b], before + 1)
                step(V.tensor_tensor(old, old, new, ALU.add), done)
                if final:
                    y = (y_out if half else y_first)[:, t * CHUNK + cols.start:t * CHUNK + cols.stop]
                    step(V.tensor_tensor(y, old, nf_row[:, at:at + width], ALU.mult))

            def updates(chunk, half, uses, g_row, task, done, final=False, tile_done=None):
                mid, end = chunk + half, chunk + 2 * half
                low(chunk + RING, n=half)
                if task == "wide_o":
                    dve.wait_ge(res_in, 32)
                dve.wait_ge(chunk_used, mid)
                for t in range(TOK):
                    update(0, t, g_row, uses[t], done, final)
                low(mid + RING, n=half - RING)
                wides_before = ("wide_o", "wide_f0", "wide_f1").index(task)
                dve.wait_ge(ahead, 2 * wides_before + 1)
                update(1, 0, g_row, side_use(task, 2)[1], done, final)
                if tile_done:
                    row_sum(0, 3 if final else 2)
                last = (g_row, side_use(task, 3)[1], done, final)
                dve.wait_ge(ahead, 2 * wides_before + 2)
                update(1, 1, *last, 0)
                if tile_done:
                    tile_done(0)
                if not tile_done:
                    low(end, n=RING - 1)
                dve.wait_ge(chunk_used, end)
                update(1, 1, *last, 1)
                if not tile_done:
                    low(end + RING - 1)
                else:
                    low(end)
                    row_sum(1, 3 if final else 2)
                    tile_done(1)

            half_reduced(8)
            half_reduced(9)
            def rstd2(t):
                r = root_of(t, 2)
                step(V.reciprocal(r, r))
                step(V.tensor_scalar(diag[:, t * P:(t + 1) * P], ident[:, :], r, None, ALU.mult), diag_done)

            updates(W_O, HALF_O, uses, g1_row, "wide_o", res_done, tile_done=rstd2)

            dve.wait_ge(spread, TOK)
            V.tensor_copy(rstd_bc[:, :], bank[0][:, 0:2 * S]).then_inc(free[0], 1)
            dve.wait_ge(free[0], uses[0] + 3)
            dve.wait_ge(free[1], uses[1] + 2)
            for q in range(G_CHUNKS):
                pair = hst[:, q * 512:(q + 1) * 512]
                if q < 4:
                    V.tensor_tensor(pair, pair, rstd_bc[:, :], ALU.mult).then_inc(res_scaled, 1)
                else:
                    b = q // 2
                    dve.wait_ge(turned, b + 1)
                    V.tensor_tensor(pair, bank[b][:, q % 2 * 512:(q % 2 + 1) * 512], rstd_bc[:, :], ALU.mult)\
                        .then_inc(free[b] if q % 2 else res_scaled, 1)
                if q:
                    h_low_part(hst, q - 1, G_CHUNKS + q - 1)
                if 0 < q < RING or q > 4:
                    low(W_O + 2 * HALF_O + q - (q > 4))
            h_low_part(hst, G_CHUNKS - 1, 2 * G_CHUNKS - 1)
            low(FFN[0][0] + G_CHUNKS - 1)
            uses = [uses[0] + 3, uses[1] + 2]

            def final_norm(t):
                r, y = root_of(t, 3), y_out[:, t * CHUNK:(t + 1) * CHUNK]
                step(V.reciprocal(r, r), rstd_done)
                step(V.tensor_scalar(y, y, r, None, ALU.mult), y_done)

            for p, groups in enumerate(PASSES):
                up, down = FFN[p]
                before = sum(PASSES[:p])

                def hidden(i, mods):
                    for c in range(2 * G_CHUNKS):
                        if not (mods and i == 0 and c < 4):
                            low(up + RING + c, 2 * G_CHUNKS, i)
                        if mods and c % 2:
                            mod(160 + 8 * i + c // 2)
                    dve.wait_ge(free[0], plus(uses[0] + 1, 1, i))
                    dve.wait_ge(chunk_used, plus(up + 2 * G_CHUNKS, 2 * G_CHUNKS, i))
                    V.tensor_tensor(f32_[:, :], bank[1][:, :], silu[:, :], ALU.mult).then_inc(free[1], 1)
                    dve.wait_ge(f_high, plus(before + 1, 1, i))
                    hid = f_hi[:, bass.ds(i * CHUNK, CHUNK)]
                    V.tensor_tensor(f_lo[:, bass.ds(i * CHUNK, CHUNK)], f32_[:, :], hid.bitcast(F32), ALU.subtract)\
                        .then_inc(f_low, 1)

                first = 0
                if p == 0:
                    first = 4
                    for i in range(first):
                        hidden(i, True)
                with dve.Fori(first, groups) as i:
                    hidden(i, False)
                uses = [n + groups for n in uses]
                if p == 0:
                    dve.wait_ge(g2_in, 16)
                    row_sums("m10", g2_row, 0)
                    row_sums("m11", g2_row, 1)
                half = groups * GROUP
                if p:
                    dve.wait_ge(nf_in, 16)
                updates(down, half, uses, g2_row, f"wide_f{p}", res_done if p else dve_order, bool(p),
                        final_norm if p else None)
                uses = [n + 1 for n in uses]


_WEIGHTS = ["w_in", "lru_w_out", "sc_w_out", "pool_w", "w_o", "ffn_w1", "ffn_w3", "ffn_w2"]


def _group(np, w, col):
    k = w.shape[0] // (2 * P)
    return w[:, col:col + 512].reshape(k, 2, P, 512).transpose(0, 2, 1, 3).reshape(k, P, CHUNK)


def _half(np, w, half):
    return w[:, half * CHUNK:(half + 1) * CHUNK].reshape(-1, P, CHUNK)


def _weight_stream(np, w):
    w_in, proj = w["w_in"], 2 * W_LRU + 4 * W_LRU
    opening = np.stack([_group(np, w_in, g * 512) for g in (0, 1, A_GROUPS)], axis=1)
    parts = [opening.reshape(-1, P, CHUNK)] + [_group(np, w_in, g * 512) for g in range(2, A_GROUPS)]
    for j in range(4):
        parts += [_group(np, w_in, proj + j * 512), _group(np, w["lru_w_out"], j * 512)]
    parts += [_group(np, w_in, (A_GROUPS + 1) * 512)]
    for j in range(4):
        parts += [_group(np, w_in, proj + D + j * 512), _group(np, w["sc_w_out"], j * 512)]
    for j in range(4):
        parts += [_group(np, w_in, proj + 2 * D + j * 512), _group(np, w["pool_w"][j], 0)]
    parts += [_half(np, w["w_o"], h) for h in range(2)]
    first = 0
    for groups in PASSES:
        for g in range(first, first + groups):
            parts += [_group(np, w["ffn_w1"], g * 512), _group(np, w["ffn_w3"], g * 512)]
        parts += [_half(np, w["ffn_w2"][first * 512:(first + groups) * 512], h) for h in range(2)]
        first += groups
    return np.concatenate(parts)


def kernel(**inputs):
    import numpy as np
    import concourse.bacc as bacc
    from concourse.bass_utils import run_bass_kernel_spmd

    a = {k: np.asarray(v) for k, v in inputs.items()}
    w_stream = _weight_stream(np, {k: a[k][0] for k in _WEIGHTS})
    assert w_stream.shape == (N_CHUNKS, P, CHUNK)
    halves = a["w_mod"][0].reshape(KT, P, 2 * len(MOD_ORDER), CHUNK).transpose(2, 0, 1, 3)
    scale_shift = a["w_mod"][0][:, :2 * D].reshape(KT // 2, 2, P, 2, KT // 2, 2 * P)[:, :, :, ::-1]
    opening = scale_shift.transpose(4, 0, 2, 1, 3, 5).reshape(-1, P, CHUNK)
    m_stream = np.concatenate([opening] + [halves[2 * v + h] for v in MOD_ORDER[2:] for h in range(2)])

    def cols(v):
        return v.reshape(-1, P).T

    params = np.ascontiguousarray(np.concatenate([
        cols(a["b_mod"]), cols(a["norm_mix"]), cols(a["norm_ffn"]), cols(a["pool_scale"]), cols(a["lru_conv_w"]),
        cols(a["lru_conv_b"]), cols(a["lru_b_a"]), cols(a["lru_b_x"]), cols(a["lru_lambda"]),
        cols(a["sc_conv_w"]), cols(a["c"]),
        cols(a["b_mod"])[:, :2 * KT].reshape(P, 2, KT // 2, 2)[:, ::-1].transpose(0, 2, 1, 3).reshape(P, 2 * KT)],
        axis=1))
    assert params.shape == (P, N_PARAM)
    gate_w = np.zeros((2, P, BT, P), np.float32)
    for n, name in enumerate(("lru_w_a", "lru_w_x")):
        for head in range(2 * BT):
            o = (head % 2) * 64
            gate_w[n, o:o + 64, head // 2, o:o + 64] = a[name][0, head]
    b_mod = a["b_mod"].reshape(-1, D)
    rows = np.ascontiguousarray(np.stack([b_mod[2], b_mod[5], a["norm_final"]]))
    pool_cnt = np.tile(np.concatenate([w / np.arange(1, w + 1) for w in POOL_WINDOWS]).astype(np.float32), (P, 1))
    arrays = {
        "x": np.ascontiguousarray(a["x"][0]), "params": params, "gate_w": gate_w.reshape(2, P, BT * P),
        "rows": rows, "pool_cnt": pool_cnt, "w_stream": w_stream, "m_stream": m_stream,
        "ident": np.eye(P, dtype=np.float32),
    }
    nc = bacc.Bacc("TRN2", target_bir_lowering=False, num_devices=1)
    args = [nc.dram_tensor(f"in_{k}", v.shape, F32, kind="ExternalInput").ap() for k, v in arrays.items()]
    out = nc.dram_tensor("out_y", (S, D), F32, kind="ExternalOutput").ap()
    trunk_kernel(nc, *args, out)
    result = run_bass_kernel_spmd(nc, [{f"in_{k}": v for k, v in arrays.items()}], core_ids=[0])
    return result.results[0]["out_y"].reshape(1, S, D)
```
